# Optimizing a Trainium2 kernel written in Bass

```python
import math
import jax
import jax.numpy as jnp
from jax import lax
import numpy as np

"""One inference step of a hybrid diffusion / flow-matching backbone (2 trunk layers).

Layer 0 (even): one combined input projection feeding two parallel head groups,
  A = chunked spatial-gating MLP (gMLP style, 8 groups x 128 ch, chunks of 128 positions)
  B = grouped-query attention (8 q heads, 2 kv heads, head_dim 128), per-head RMS-normed q/k,
      2-D axial rotary positions on latent tokens, bidirectional,
  each branch multiplied by its own SiLU gate path, outputs concatenated into one output projection.
Layer 1 (odd): differential attention (16 heads, q/k 2x64, v 128) with learned lambda,
  per-head RMSNorm and (1 - lambda_init) scaling, SiLU gate path, output projection.
Every sub-layer: RMSNorm pre-norm + adaLN (shift, scale, gate from SiLU(cond) @ W + b), residual add.
Final RMSNorm. Context tokens use cond = c_ctx and read only context tokens; latent tokens use
cond = c and read latent tokens plus all cached context keys in one softmax.

Inputs:
  x_prompt (BATCH, SEQ, D_MODEL)            context tokens of new requests
  x_sample (DEC_BATCH, DEC_SEQ, D_MODEL)    noisy latent tokens (grid width GRID_W)
  cache_k0 (DEC_BATCH, PAST_LEN, B_KV_HEADS, B_HEAD_DIM)   layer-0 context keys (RMS-normed, no rotary)
  cache_v0 (DEC_BATCH, PAST_LEN, B_KV_HEADS, B_HEAD_DIM)   layer-0 context values
  cache_k1 (DEC_BATCH, PAST_LEN, C_HEADS, 2, C_QK_DIM)     layer-1 context keys (both maps)
  cache_v1 (DEC_BATCH, PAST_LEN, C_HEADS, C_V_DIM)         layer-1 context values
  c (DEC_BATCH, D_MODEL), c_ctx (D_MODEL,), then weights.
Output tuple:
  (y_prompt (BATCH, SEQ, D_MODEL), y_sample (DEC_BATCH, DEC_SEQ, D_MODEL),
   new_k0 (BATCH, SEQ, B_KV_HEADS, B_HEAD_DIM), new_v0 (BATCH, SEQ, B_KV_HEADS, B_HEAD_DIM),
   new_k1 (BATCH, SEQ, C_HEADS, 2, C_QK_DIM), new_v1 (BATCH, SEQ, C_HEADS, C_V_DIM))
"""

D_MODEL = 2048
BATCH = 1
SEQ = 128
DEPTH = 2
DEC_BATCH = 1
DEC_SEQ = 512
PAST_LEN = 128

GRID_W = 64
QBLOCK = 128
CHUNK = 128
ROPE_THETA = 10000.0
EPS = 1e-6

A_GROUPS = 8
A_GROUP_CH = 128
A_WIDTH = A_GROUPS * A_GROUP_CH
B_HEADS = 8
B_KV_HEADS = 2
B_HEAD_DIM = 128
B_GROUP = B_HEADS // B_KV_HEADS
B_WIDTH = B_HEADS * B_HEAD_DIM
B_KV_WIDTH = B_KV_HEADS * B_HEAD_DIM
IN0_WIDTH = 3 * A_WIDTH + 2 * B_WIDTH + 2 * B_KV_WIDTH
OUT0_WIDTH = A_WIDTH + B_WIDTH
C_HEADS = 16
C_QK_DIM = 64
C_V_DIM = 2 * C_QK_DIM
C_QK_WIDTH = C_HEADS * 2 * C_QK_DIM
C_V_WIDTH = C_HEADS * C_V_DIM
IN1_WIDTH = 2 * C_QK_WIDTH + 2 * C_V_WIDTH
LAMBDA_INIT_1 = 0.8 - 0.6 * math.exp(-0.3 * 1)

kernel_name = "hybrid_gmlp_gqa_diffattn_dit_step"

F32 = jnp.float32

def rms_norm(x, g):
    xf = x.astype(F32)
    xf = xf * lax.rsqrt(jnp.mean(xf * xf, axis=-1, keepdims=True) + EPS)
    return (xf * g.astype(F32)).astype(x.dtype)

def ada_modulate(x, cond, w_ada, b_ada, norm_g):
    mod = jax.nn.silu(cond) @ w_ada + b_ada
    if mod.ndim == 1:
        mod = mod[None]
    shift, scale, gate = jnp.split(mod[:, None, :], 3, axis=-1)
    h = rms_norm(x, norm_g) * (1 + scale) + shift
    return h, gate

def rope_1d(x, pos):
    half = x.shape[-1] // 2
    freqs = ROPE_THETA ** (-jnp.arange(half, dtype=F32) / half)
    ang = pos[:, None] * freqs[None, :]
    shp = (pos.shape[0],) + (1,) * (x.ndim - 3) + (half,)
    cos = jnp.cos(ang).reshape(shp)
    sin = jnp.sin(ang).reshape(shp)
    xf = x.astype(F32)
    x1, x2 = xf[..., :half], xf[..., half:]
    return jnp.concatenate([x1 * cos - x2 * sin, x1 * sin + x2 * cos], axis=-1).astype(x.dtype)

def rope_2d(x, row, col):
    h = x.shape[-1] // 2
    return jnp.concatenate([rope_1d(x[..., :h], row), rope_1d(x[..., h:], col)], axis=-1)

def over_query_blocks(fn, q):
    b_, t = q.shape[0], q.shape[1]
    nb = t // QBLOCK
    qb = jnp.moveaxis(q.reshape((b_, nb, QBLOCK) + q.shape[2:]), 1, 0)
    out = lax.map(fn, qb)
    return jnp.moveaxis(out, 0, 1).reshape((b_, t) + out.shape[3:])

def gqa_attend(q, k, v):
    scale = B_HEAD_DIM ** -0.5

    def block(qb):
        s = jnp.einsum('bqhgd,bshd->bhgqs', qb, k).astype(F32) * scale
        p = jax.nn.softmax(s, axis=-1).astype(v.dtype)
        return jnp.einsum('bhgqs,bshd->bqhgd', p, v)

    return over_query_blocks(block, q)

def diff_attend(q, k, v, lam):
    scale = C_QK_DIM ** -0.5

    def block(qb):
        s = jnp.einsum('bqhmd,bshmd->bhmqs', qb, k).astype(F32) * scale
        p = jax.nn.softmax(s, axis=-1)
        w = (p[:, :, 0] - lam * p[:, :, 1]).astype(v.dtype)
        return jnp.einsum('bhqs,bshe->bqhe', w, v)

    return over_query_blocks(block, q)

def chunk_spatial_gate(u, v, w_s, b_s):
    b_, t = u.shape[0], u.shape[1]
    n = t // CHUNK
    vf = v.astype(F32)
    mu = jnp.mean(vf, axis=-1, keepdims=True)
    var = jnp.mean((vf - mu) ** 2, axis=-1, keepdims=True)
    vn = ((vf - mu) * lax.rsqrt(var + EPS)).astype(v.dtype)
    vc = vn.reshape(b_, n, CHUNK, A_GROUPS, A_GROUP_CH)
    s = jnp.einsum('gpq,bnqgc->bnpgc', w_s, vc) + b_s.T[None, None, :, :, None]
    return u * s.reshape(b_, t, A_WIDTH)

def mixer_ab(h, w_in, w_s, b_s, q_g, k_g, w_out, pos, ctx_k, ctx_v):
    b_, t = h.shape[0], h.shape[1]
    z = h @ w_in
    idx = np.cumsum([A_WIDTH, A_WIDTH, A_WIDTH, B_WIDTH, B_KV_WIDTH, B_KV_WIDTH]).tolist()
    u_a, v_a, g_a, q, k, v, g_b = jnp.split(z, idx, axis=-1)
    y_a = chunk_spatial_gate(u_a, v_a, w_s, b_s) * jax.nn.silu(g_a)
    q = rms_norm(q.reshape(b_, t, B_KV_HEADS, B_GROUP, B_HEAD_DIM), q_g)
    k = rms_norm(k.reshape(b_, t, B_KV_HEADS, B_HEAD_DIM), k_g)
    v = v.reshape(b_, t, B_KV_HEADS, B_HEAD_DIM)
    if pos is None:
        qr, k_all, v_all = q, k, v
    else:
        row, col = pos
        qr = rope_2d(q, row, col)
        k_all = jnp.concatenate([rope_2d(k, row, col), ctx_k], axis=1)
        v_all = jnp.concatenate([v, ctx_v], axis=1)
    y_b = gqa_attend(qr, k_all, v_all).reshape(b_, t, B_WIDTH) * jax.nn.silu(g_b)
    out = jnp.concatenate([y_a, y_b], axis=-1) @ w_out
    return out, k, v

def mixer_diff(h, w_in, lq1, lk1, lq2, lk2, sub_g, w_out, pos, ctx_k, ctx_v):
    b_, t = h.shape[0], h.shape[1]
    z = h @ w_in
    idx = [C_QK_WIDTH, 2 * C_QK_WIDTH, 2 * C_QK_WIDTH + C_V_WIDTH]
    q, k, v, g = jnp.split(z, idx, axis=-1)
    q = q.reshape(b_, t, C_HEADS, 2, C_QK_DIM)
    k = k.reshape(b_, t, C_HEADS, 2, C_QK_DIM)
    v = v.reshape(b_, t, C_HEADS, C_V_DIM)
    lam = (jnp.exp(jnp.sum(lq1.astype(F32) * lk1.astype(F32)))
           - jnp.exp(jnp.sum(lq2.astype(F32) * lk2.astype(F32))) + LAMBDA_INIT_1)
    if pos is None:
        qr, k_all, v_all = q, k, v
    else:
        row, col = pos
        qr = rope_2d(q, row, col)
        k_all = jnp.concatenate([rope_2d(k, row, col), ctx_k], axis=1)
        v_all = jnp.concatenate([v, ctx_v], axis=1)
    o = diff_attend(qr, k_all, v_all, lam)
    o = rms_norm(o, sub_g) * (1 - LAMBDA_INIT_1)
    out = (o.reshape(b_, t, C_V_WIDTH) * jax.nn.silu(g)) @ w_out
    return out, k, v

def setup_inputs(seed: int = 0) -> dict:
    key = jax.random.key(seed)
    ks = jax.random.split(key, 32)
    D = D_MODEL

    def nrm(k, shape, s):
        return jax.random.normal(k, shape, F32) * s

    return {
        "x_prompt": nrm(ks[0], (BATCH, SEQ, D), 1.0),
        "x_sample": nrm(ks[1], (DEC_BATCH, DEC_SEQ, D), 1.0),
        "cache_k0": nrm(ks[2], (DEC_BATCH, PAST_LEN, B_KV_HEADS, B_HEAD_DIM), 1.0),
        "cache_v0": nrm(ks[3], (DEC_BATCH, PAST_LEN, B_KV_HEADS, B_HEAD_DIM), 1.0),
        "cache_k1": nrm(ks[4], (DEC_BATCH, PAST_LEN, C_HEADS, 2, C_QK_DIM), 1.0),
        "cache_v1": nrm(ks[5], (DEC_BATCH, PAST_LEN, C_HEADS, C_V_DIM), 1.0),
        "c": nrm(ks[6], (DEC_BATCH, D), 1.0),
        "c_ctx": nrm(ks[7], (D,), 1.0),
        "w_ada0": nrm(ks[8], (D, 3 * D), D ** -0.5),
        "b_ada0": nrm(ks[9], (3 * D,), 0.02),
        "norm_g0": 1.0 + nrm(ks[10], (D,), 0.02),
        "w_in0": nrm(ks[11], (D, IN0_WIDTH), D ** -0.5),
        "w_s0": nrm(ks[12], (A_GROUPS, CHUNK, CHUNK), CHUNK ** -0.5),
        "b_s0": nrm(ks[13], (A_GROUPS, CHUNK), 0.02),
        "q_norm_g0": 1.0 + nrm(ks[14], (B_HEAD_DIM,), 0.02),
        "k_norm_g0": 1.0 + nrm(ks[15], (B_HEAD_DIM,), 0.02),
        "w_out0": nrm(ks[16], (OUT0_WIDTH, D), OUT0_WIDTH ** -0.5),
        "w_ada1": nrm(ks[17], (D, 3 * D), D ** -0.5),
        "b_ada1": nrm(ks[18], (3 * D,), 0.02),
        "norm_g1": 1.0 + nrm(ks[19], (D,), 0.02),
        "w_in1": nrm(ks[20], (D, IN1_WIDTH), D ** -0.5),
        "lambda_q1": nrm(ks[21], (C_QK_DIM,), 0.1),
        "lambda_k1": nrm(ks[22], (C_QK_DIM,), 0.1),
        "lambda_q2": nrm(ks[23], (C_QK_DIM,), 0.1),
        "lambda_k2": nrm(ks[24], (C_QK_DIM,), 0.1),
        "subln_g1": 1.0 + nrm(ks[25], (C_V_DIM,), 0.02),
        "w_out1": nrm(ks[26], (C_V_WIDTH, D), C_V_WIDTH ** -0.5),
        "final_g": 1.0 + nrm(ks[27], (D,), 0.02),
    }

def reference(x_prompt, x_sample, cache_k0, cache_v0, cache_k1, cache_v1, c, c_ctx,
              w_ada0, b_ada0, norm_g0, w_in0, w_s0, b_s0, q_norm_g0, k_norm_g0, w_out0,
              w_ada1, b_ada1, norm_g1, w_in1, lambda_q1, lambda_k1, lambda_q2, lambda_k2,
              subln_g1, w_out1, final_g):
    ada_params = [(w_ada0, b_ada0, norm_g0), (w_ada1, b_ada1, norm_g1)]
    caches = [(cache_k0, cache_v0), (cache_k1, cache_v1)]

    def run_mixer(layer, h, pos, ctx_k, ctx_v):
        if layer % 2 == 0:
            return mixer_ab(h, w_in0, w_s0, b_s0, q_norm_g0, k_norm_g0, w_out0, pos, ctx_k, ctx_v)
        return mixer_diff(h, w_in1, lambda_q1, lambda_k1, lambda_q2, lambda_k2, subln_g1, w_out1,
                          pos, ctx_k, ctx_v)

    x = x_prompt
    ctx_state = []
    for layer in range(DEPTH):
        w_ada, b_ada, ng = ada_params[layer]
        h, gate = ada_modulate(x, c_ctx, w_ada, b_ada, ng)
        out, k_ctx, v_ctx = run_mixer(layer, h, None, None, None)
        x = x + gate * out
        ctx_state.append((k_ctx, v_ctx))
    y_prompt = rms_norm(x, final_g)

    t = x_sample.shape[1]
    rows = t // GRID_W
    row_pos = jnp.repeat(jnp.arange(rows, dtype=F32), GRID_W)
    col_pos = jnp.tile(jnp.arange(GRID_W, dtype=F32), rows)
    pos = (row_pos, col_pos)
    x = x_sample
    for layer in range(DEPTH):
        w_ada, b_ada, ng = ada_params[layer]
        h, gate = ada_modulate(x, c, w_ada, b_ada, ng)
        ck, cv = caches[layer]
        out, _, _ = run_mixer(layer, h, pos, ck, cv)
        x = x + gate * out
    y_sample = rms_norm(x, final_g)

    (new_k0, new_v0), (new_k1, new_v1) = ctx_state
    return (y_prompt, y_sample, new_k0, new_v0, new_k1, new_v1)


_drawn_inputs = setup_inputs


def setup_inputs(seed=0):
    import zlib

    import numpy as np

    out = dict(_drawn_inputs(seed))
    spreads = {}
    factors = {'cache_k0': 6.216,
     'cache_v0': 5.251,
     'norm_g0': 3.244,
     'b_s0': 6.481,
     'q_norm_g0': 8.0,
     'k_norm_g0': 2.832,
     'norm_g1': 3.269,
     'lambda_q1': 8.0,
     'lambda_k1': 8.0,
     'lambda_q2': 2.668,
     'subln_g1': 30.908,
     'final_g': 7.99,
     'cache_k1': 8.0,
     'cache_v1': 8.0}
    for name, (base, spread) in spreads.items():
        noise = np.random.default_rng([zlib.crc32(name.encode()), seed]).standard_normal(out[name].shape)
        drawn = base * np.exp(spread * noise) if base else spread * noise
        out[name] = jnp.asarray(drawn.astype(out[name].dtype))
    for name, factor in factors.items():
        out[name] = (out[name] * factor).astype(out[name].dtype)
    return out
```

```python
import math
from contextlib import ExitStack

import concourse.bass as bass
from concourse import mybir

F32 = mybir.dt.float32
F32R = mybir.dt.float32r
I32 = mybir.dt.int32
ACT = mybir.ActivationFunctionType
ALU = mybir.AluOpType
AX_X = mybir.AxisListType.X

P = 128
D = 2048
KT = D // P
NC = 512
TS, TT = 4, 5
NTOK = TT * P
EPS = 1e-6
UNITS = KT // 2
RAW = 8
RING = 4
AHEAD = 2
FEED = 3
W_CREDIT = RING
ACC_CREDIT = 1
N_SETUP = 6 + 3 + 3 + 4 + 2
LAMBDA_INIT = 0.8 - 0.6 * math.exp(-0.3)

C_ADA0 = 0
C_L0 = 8
C_L0I = 11
C_O0 = 27
C_L1 = 35
C_O1 = 51

SLOTS = KT * TT

ORDER0 = ["T", "T", "T", "S", "S", "T", "S", "T", "T", "S", "P", "S", "B", "T", "T", "T", "P", "B", "T", "P", "B"]
ORDER1 = ["T", "T", "T", "S", "S", "S", "S", "T", "S", "T", "S", "T", "S", "P", "S", "B", "S", "T", "S",
          "T", "T", "P", "B", "T", "P", "B"]
AT0 = [0, 3, 6, 9, 13, 17, 19, 22, 25, 28, 31, 33, 36, 38, 41, 44, 47, 49, 51, 53, 56]
AT1 = [0, 2, 4, 7, 11, 15, 20, 24, 26, 28, 31, 32, 35, 37, 40, 41, 44, 46, 49, 50, 52, 54, 56, 57, 58, 59]
SPATIAL = ["L", "G", "G"]


class Layer:

    def __init__(self, n, heads, maps, order):
        self.order = order
        self.n, self.heads, self.maps = n, heads, maps
        self.dk = P // maps
        self.scale = self.dk ** -0.5
        self.n_scores = maps * TT
        self.n_turn = 10
        self.n_bank = 13


def chain(parts):
    for part in parts:
        yield from part


def kernel_program(nc, a, outs):
    L0, L1 = Layer(0, 8, 1, ORDER0), Layer(1, 16, 2, ORDER1)
    y_prompt, y_sample, new_k0, new_v0, new_k1, new_v1 = outs

    ctx = ExitStack()
    with ctx:
        def sb(name, shape, dt=F32):
            return ctx.enter_context(nc.sbuf_tensor(name, shape, dt))

        def sem(name):
            return ctx.enter_context(nc.semaphore(name))

        hT_hi = sb("hT_hi", [P, KT, NTOK], F32R)
        hT_lo = sb("hT_lo", [P, KT, NTOK], F32R)
        w_raw = sb("w_raw", [P, RAW, 2, NC])
        w_hi = sb("w_hi", [P, RING, NC], F32R)
        w_lo = sb("w_lo", [P, RING, NC], F32R)
        stage = sb("stage", [P, TT, NC])
        rope_c = sb("rope_c", [P, TS * P])
        rope_s = sb("rope_s", [P, TS * P])
        consts = sb("consts", [P, 386])
        ident = consts[:, 0:128]
        sel_row = [consts[0:4, 128:256], consts[0:4, 256:384]]
        sel_col = consts[0:4, 384:386]
        vcol = sb("vcol", [P, P])
        cst = sb("cst", [P, KT * 4 + P], F32R)
        modrow = sb("modrow", [4, NC])
        modcol = [sb(f"modcol{l}", [P, 32, 2]) for l in range(2)]
        gq = sb("gq", [P, P])
        gk = sb("gk", [P, P])
        gsub = sb("gsub", [P, P])
        bsT = sb("bsT", [P, 8])
        small = sb("small", [P, 96])
        work = sb("work", [P, 3 * D])
        taken = [0]

        def part(*shape):
            n = math.prod(shape)
            at = work[:, taken[0]:taken[0] + n]
            taken[0] += n
            return at if len(shape) == 1 else at.rearrange("p (a b) -> p a b", b=shape[1])

        q_in = part(TT, P)
        k_in = part(TT, P)
        v_in = part(TT, P)
        ck_in = part(P)
        cv_in = part(P)
        rope_b = part(TS * P)
        weights = part(4, 640)
        o_head = part(TT, P)
        area = work[:, :].rearrange("p (a n) -> p a n", a=3)
        lam4 = area[:, 1, 1024:1280].rearrange("p (n d) -> p n d", n=4)
        rope_a = sb("rope_a", [P, TS * P])
        qT = [sb("qT_hi", [P, NTOK], F32R), sb("qT_lo", [P, NTOK], F32R)]
        kT = [sb("kT_hi", [P, NTOK + P], F32R), sb("kT_lo", [P, NTOK + P], F32R)]
        vv = [sb("v_hi", [P, TT + 1, P], F32R), sb("v_lo", [P, TT + 1, P], F32R)]
        wT = [sb("wT_hi", [P, 5, 256], F32R), sb("wT_lo", [P, 5, 256], F32R)]
        oT = sb("oT", [P, 256])

        blk = [work[:, n * TT * NC:(n + 1) * TT * NC].rearrange("p (t n) -> p t n", t=TT) for n in range(2)]
        x_old = blk[0]
        gate_b = work[:, 2 * TT * NC:(2 * TT + 2) * NC].rearrange("p (k n) -> p k n", k=2)
        gate_bias = rope_a[:, :]
        ws_t = sb("ws_t", [P, 1024])
        sp_buf = stage[:, 0:4, :].rearrange("p t n -> p (t n)")
        h5 = work[:, 5120:5120 + NTOK]
        junk = wT[0][:, 0:2, :].rearrange("p k q -> p (k q)")
        ssq = sb("ssq", [P, 20])
        rstd = sb("rstd", [P, TT])
        wts_p = sb("wts_p", [P, P])
        sums = ssq[:, 0:10]
        inv_sums = ssq[:, 10:20]
        squares = [weights[:, n, :].rearrange("p (t d) -> p t d", t=TT) for n in (0, 3)]

        ps = ctx.enter_context(nc.psum_tensor("ps", [P, 8, NC], F32))
        TURN = 5
        SC = 6
        turned = ps[:, TURN:TURN + 2, :].rearrange("p a b -> p (a b)")[:, 0:NTOK]

        def dram(name, shape):
            return nc.dram_tensor(name, shape, F32, kind="Internal").ap()

        z_d = [dram("z0", (11, P, TT, NC)), dram("z1", (16, P, TT, NC))]
        o_d = [dram("o0", (TT, P, D)), dram("o1", (TT, P, D))]
        kn_d = dram("kn", (L0.heads, P, P))
        x_d = dram("x1", (TT, P, D))
        x2_d = dram("x2", (TT, P, D))

        w_landed = [sem(f"w_landed{i}") for i in range(RAW)]
        raw_free = sem("raw_free")
        raw_taken = sem("raw_taken")
        pool_passed = sem("pool_passed")
        w_hi_ready = sem("w_hi_ready")
        w_lo_ready = sem("w_lo_ready")
        w_used = sem("w_used")
        acc_ready = sem("acc_ready")
        acc_free = sem("acc_free")
        stage_full = sem("stage_full")
        stage_stored = sem("stage_stored")
        stage_free = sem("stage_free")
        row_ready = sem("row_ready")
        mod_ready = sem("mod_ready")
        setup_in = sem("setup_in")
        setup_pe = sem("setup_pe")
        setup_act = sem("setup_act")
        setup_dve = sem("setup_dve")
        xt_in = sem("xt_in")
        sq_done = sem("sq_done")
        out_done = sem("out_done")
        x_in = [sem(f"x_in{n}") for n in range(2)]
        o_in = [sem(f"o_in{n}") for n in range(2)]
        g_in = sem("g_in")
        tanh_done = sem("tanh_done")
        src_ready = sem("src_ready")
        turn_ready = sem("turn_ready")
        turn_mid = sem("turn_mid")
        turn_hi = sem("turn_hi")
        turn_free = sem("turn_free")
        sp_in = sem("sp_in")
        vn_ready = sem("vn_ready")
        sp_ready = sem("sp_ready")
        sp_free = sem("sp_free")
        sp_stored = sem("sp_stored")
        gb_in = sem("gb_in")
        gb_free = sem("gb_free")
        xo_in = sem("xo_in")
        xo_free = sem("xo_free")
        kn_stored = sem("kn_stored")
        fg_in = sem("fg_in")
        fin_in = [sem(f"fin_in{n}") for n in range(2)]
        fin_ready = sem("fin_ready")
        fin_stored = sem("fin_stored")
        copied = sem("copied")

        class AttnSems:
            def __init__(self, l):
                s = lambda n: sem(f"{n}_{l}")
                self.qk_in = s("qk_in")
                self.v_in = s("v_in")
                self.normed = s("head_normed")
                self.roped = s("head_roped")
                self.t_ready = s("t_ready")
                self.t_hi = s("t_hi")
                self.t_free = s("t_free")
                self.v_hi = s("v_hi")
                self.v_split = s("v_split")
                self.s_ready = s("s_ready")
                self.s_max = s("s_max")
                self.s_exp = s("s_exp")
                self.w_ready = s("w_ready")
                self.pv_ready = s("pv_ready")
                self.pv_copied = s("pv_copied")
                self.b_ready = s("b_ready")
                self.o_done = s("o_done")
                self.o_stored = s("o_stored")
                self.o_free = s("o_free")

        S = [AttnSems(0), AttnSems(1)]
        block = ctx.enter_context(nc.Block())

        w_units = {}

        def unit(name, i):
            if name not in w_units:
                w_units[name] = a[name].rearrange("(u k p) n -> u p k n", k=2, p=P)
            return w_units[name][i]

        @block.sync
        def _(sp):
            def load_chunk(c, name, col):
                for i in range(UNITS):
                    sp.wait_ge(raw_free, c * UNITS + (i + 1))
                    sp.sem_inc(raw_taken, 1)
                    sp.dma_start(w_raw[:, i % RAW, :, :], unit(name, i)[:, :, bass.ds(col, NC)]).then_inc(
                        w_landed[i % RAW], 16)

            rows = [("c", 0, 16, "o (r d) -> (o r) d"), ("c_ctx", 16, 16, "(r d) -> r d"),
                    ("norm_g0", 32, 16, "(r d) -> r d"), ("norm_g1", 48, 16, "(r d) -> r d")]
            for name, at, n, how in rows:
                sp.dma_start(area[at:at + n, 0, 0:P], a[name].rearrange(how, d=P)).then_inc(setup_in, 16)
            for l in range(2):
                sp.dma_start(area[64 + 32 * l:96 + 32 * l, 0, 0:P],
                             a[f"b_ada{l}"][0:2 * D].rearrange("(r d) -> r d", d=P)).then_inc(setup_in, 16)
            sp.dma_start(consts[:, :], a["layout"][:, 0:386]).then_inc(setup_in, 16)
            sp.dma_start(rope_c[:, :], a["rope"][0, 0]).then_inc(setup_in, 16)
            sp.dma_start(rope_s[:, :], a["rope"][0, 1]).then_inc(setup_in, 16)
            for t, name in ((gq, "q_norm_g0"), (gk, "k_norm_g0"), (gsub, "subln_g1")):
                sp.dma_start(t[:, :], a[name].unsqueeze(0).to_broadcast([P, P])).then_inc(setup_in, 16)
            for n, name in enumerate(("lambda_q1", "lambda_k1", "lambda_q2", "lambda_k2")):
                sp.dma_start(lam4[:, n, :], a[name].unsqueeze(0).to_broadcast([P, 64])).then_inc(setup_in, 16)
            sp.dma_start(area[0:8, 0, P:2 * P], a["b_s0"]).then_inc(setup_in, 16)
            sp.dma_start(area[:, 1, 0:1024].rearrange("p (g q) -> p g q", g=8),
                         a["w_s0"].rearrange("g p q -> p g q")).then_inc(setup_in, 16)

            with sp.Fori(0, 8) as i:
                load_chunk(i, "w_ada0", i * NC)
            load_chunk(C_L0, "w_in0", 4096)
            with sp.Fori(0, 2) as i:
                load_chunk(i + (C_L0 + 1), "w_in0", i * NC + 3072)
            with sp.Fori(0, 8) as i:
                load_chunk(i * 2 + C_L0I, "w_in0", i * NC + (i // 6) * 1536)
                load_chunk(i * 2 + (C_L0I + 1), "w_ada1", i * NC)
            with sp.Fori(0, 4) as j:
                load_chunk(j * 2 + C_O0, "w_ada0", j * NC + 2 * D)
                load_chunk(j * 2 + (C_O0 + 1), "w_out0", j * NC)
            with sp.Fori(0, 4) as g:
                for n in range(3):
                    load_chunk(g * 3 + (C_L1 + n), "w_in1", g * NC + n * D)
            with sp.Fori(0, 4) as i:
                load_chunk(i + (C_L1 + 12), "w_in1", i * NC + 3 * D)
            with sp.Fori(0, 4) as j:
                load_chunk(j * 2 + C_O1, "w_ada1", j * NC + 2 * D)
                load_chunk(j * 2 + (C_O1 + 1), "w_out1", j * NC)

        class Pace:

            def __init__(self, at, per):
                self.at, self.per = at, per

            def due(self, slot):
                return sum(1 for x in self.at if x == slot % self.per)

            def due_in(self, n, kt):
                return sum(self.due(n * SLOTS + kt * TT + t) for t in range(TT))

        pace0 = Pace(AT0, SLOTS)
        pace0s = Pace(AT0 + [60, 65, 70], SLOTS)
        pace0t = Pace([x * 7 // 8 for x in AT0] + [52, 56, 61, 66, 70, 75], SLOTS)
        pace1 = Pace(AT1, 60)
        pace1g = Pace([x * 6 // 5 for x in AT1] + [71, 72, 73, 74, 76, 77, 78], SLOTS)

        def wait_slot_used(eng, c, kt):
            k = kt - RING
            if k >= 0:
                eng.wait_ge(w_used, c * 15 + (k + 1 + W_CREDIT))
            elif k == -1:
                eng.wait_ge(acc_ready, c * 5 + ACC_CREDIT)
            else:
                eng.wait_ge(w_used, (c - 1) * 15 + (KT + k + 1 + W_CREDIT))

        def attention_pe(pe, L, h, tiles=()):
            s = S[L.n]
            NT, NS, NF = L.n_turn, L.n_scores, L.n_bank

            def turn(q, blocks):
                pe.wait_ge(s.t_free, h * NF + (q + 1))
                for n, src in enumerate(blocks):
                    last = nc.tensor.transpose(ps[:, TURN, n * P:(n + 1) * P], src, ident)
                last.then_inc(s.t_ready, 1)

            def scores(n, q0, halves):
                r0 = (n % L.maps) * L.dk
                pe.wait_ge(s.s_exp, h * NS + (n + 1))
                for b, (k0, w) in enumerate(halves):
                    for i, (x, y) in enumerate(((0, 0), (0, 1), (1, 0))):
                        last = nc.tensor.matmul(ps[:, SC + b, 0:w], qT[x][r0:r0 + L.dk, q0:q0 + P],
                                                kT[y][r0:r0 + L.dk, k0:k0 + w], start=(i == 0), stop=(i == 2))
                last.then_inc(s.s_ready, 1)

            def products(q, width, tiles):
                pe.wait_ge(s.t_free, h * NF + (q + 1))
                for k, vt in enumerate(tiles):
                    for i, (x, y) in enumerate(((0, 0), (0, 1), (1, 0))):
                        last = nc.tensor.matmul(ps[:, TURN, 0:width], vv[x][:, vt, :], wT[y][:, k, 0:width],
                                                start=(k == 0 and i == 0), stop=(k == len(tiles) - 1 and i == 2))
                last.then_inc(s.pv_ready, 1)

            def back(n, count):
                pe.wait_ge(s.pv_copied, h * 3 + (n + 1))
                for i in range(count):
                    last = nc.tensor.transpose(ps[:, TURN, i * P:(i + 1) * P], oT[:, i * P:(i + 1) * P], ident)
                last.then_inc(s.b_ready, 1)

            r = n = p = b = q = 0
            for kind in L.order:
                if kind == "T":
                    if r == 0:
                        pe.wait_ge(s.roped, h + 1)
                        blocks = [q_in[:, t, :] for t in range(TS)]
                    elif r == 1:
                        blocks = [k_in[:, t, :] for t in range(TS)]
                    elif r == 2:
                        blocks = [q_in[:, TS, :], ck_in, k_in[:, TS, :]]
                    elif r < 9:
                        tile = 2 * (r // 3 - 1)
                        if r % 3 == 0:
                            if L.maps == 1:
                                pe.wait_ge(s.s_exp, h * NS + (tile + 3))
                            else:
                                pe.wait_ge(s.w_ready, h * 5 + (tile + 3))
                        at = tile if L.maps == 1 else 2
                        blocks = [weights[:, at + i, k * P:(k + 1) * P] for k in ((0, 1), (2, 3), (4,))[r % 3]
                                  for i in range(2)]
                    else:
                        if L.maps == 1:
                            pe.wait_ge(s.s_exp, h * NS + 6)
                        else:
                            pe.wait_ge(s.w_ready, h * 5 + 6)
                        blocks = [wts_p[:, :]]
                    turn(q, blocks)
                    r, q = r + 1, q + 1
                elif kind == "S":
                    if n == 0:
                        pe.wait_ge(s.t_free, h * NF + 4)
                    if n < TS * L.maps:
                        scores(n, n // L.maps * P, ((0, 320), (320, 320)))
                    else:
                        scores(n, TS * P, ((NTOK, P),))
                    n += 1
                elif kind == "P":
                    if p == 0:
                        pe.wait_ge(s.v_split, h + 1)
                    if p < 2:
                        products(q, 256, [0, 1, 2, 3, 5])
                    else:
                        products(q, P, [4])
                    p += 1
                else:
                    back(b, 2 if b < 2 else 1)
                    b, q = b + 1, q + 1
                yield
            for x, tile in enumerate(tiles):
                pe.wait_ge(vn_ready, tile + 1)
                yield
                for half in range(2):
                    if half == 0 and x == 0:
                        pe.wait_ge(s.t_free, h * NF + (NF + 1))
                    else:
                        pe.wait_ge(sp_free, tile * 2 + half)
                    for g in range(4):
                        at = (half * 4 + g) * P
                        last = nc.tensor.matmul(ps[:, TURN, g * P:(g + 1) * P], ws_t[:, at:at + P],
                                                sp_buf[:, at:at + P], start=True, stop=True)
                    last.then_inc(sp_ready, 1)
                    yield

        @block.tensor
        def _(pe):
            def feed_turn(F, kt):
                if kt % 4 == 0:
                    pe.wait_ge(src_ready, 4 * F + kt // 4 + 1)
                if kt > 0 and F % 2 == 0:
                    pe.wait_ge(turn_mid, 8 * F + kt)
                elif kt > 0:
                    pe.wait_ge(turn_free, 16 * F + kt)
                for t in range(TT):
                    last = nc.tensor.transpose(ps[:, TURN + t // TS, t % TS * P:(t % TS + 1) * P],
                                               blk[kt // 4 % 2][:, t, kt % 4 * P:(kt % 4 + 1) * P], ident)
                last.then_inc(turn_ready, 1)

            def project_chunk(c, step=None, F=None):
                if F is not None:
                    for kt in range(FEED):
                        feed_turn(F, kt)
                for kt in range(KT):
                    if F is not None:
                        if kt + FEED < KT:
                            feed_turn(F, kt + FEED)
                        pe.wait_ge(turn_free, 16 * F + kt + 1)
                    pe.wait_ge(w_lo_ready, c * KT + (kt + 1))
                    for t in range(TT):
                        if kt == 0:
                            pe.wait_ge(acc_free, c * 5 + (t + 1))
                        for i, (x, w) in enumerate(((hT_hi, w_hi), (hT_hi, w_lo), (hT_lo, w_hi))):
                            last = nc.tensor.matmul(ps[:, t, :], x[:, kt, t * P:(t + 1) * P], w[:, kt % RING, :],
                                                    start=(kt == 0 and i == 0), stop=(kt == KT - 1 and i == 2))
                        if kt == KT - 1:
                            last.then_inc(acc_ready, 1)
                        elif t == TT - 1:
                            last.then_inc(w_used, 1)
                        if step is not None:
                            step(kt * TT + t)

            def ada_chunk(c, n, gate):
                pe.wait_ge(acc_free, c * 5 + 5)
                for kt in range(KT):
                    pe.wait_ge(w_lo_ready, c * KT + (kt + 1))
                    for i, w in enumerate((w_hi, w_lo)):
                        last = nc.tensor.matmul(ps[:, 0, :], cst[:, kt * 4:kt * 4 + P], w[:, kt % RING, :],
                                                start=(kt == 0 and i == 0), stop=(kt == KT - 1 and i == 1))
                    last.then_inc(*((acc_ready, 5) if kt == KT - 1 else (w_used, 1)))
                pe.wait_ge(row_ready, n + 1)
                if gate:
                    for k in range(2):
                        last = nc.tensor.matmul(ps[:, 1 + k, :], sel_row[k], modrow[:, :], start=True, stop=True)
                else:
                    for k in range(4):
                        last = nc.tensor.matmul(ps[:, 1, 2 * k:2 * k + 2], modrow[:, k * P:(k + 1) * P], sel_col,
                                                start=True, stop=True)
                last.then_inc(mod_ready, 1)

            def stepper(steps, pace, n=0):
                def step(slot):
                    for _ in range(pace.due(n * SLOTS + slot)):
                        next(steps, None)
                return step

            def finish(steps):
                for _ in steps:
                    pass

            pe.sem_inc(w_used, W_CREDIT)
            pe.sem_inc(acc_ready, ACC_CREDIT)
            pe.wait_ge(setup_in, 16 * N_SETUP)
            nc.tensor.transpose(ps[:, 7, 0:P], area[:, 0, 0:P], ident)
            nc.tensor.transpose(ps[:, 7, P:P + 8], area[0:8, 0, P:2 * P], ident[0:8, 0:8])
            for g in range(8):
                last = nc.tensor.transpose(ps[:, 5 + g // 4, (g % 4) * P:(g % 4 + 1) * P],
                                           area[:, 1, g * P:(g + 1) * P], ident)
            last.then_inc(setup_pe, 1)
            pe.wait_ge(setup_dve, 1)
            with pe.Fori(0, 8) as i:
                ada_chunk(i, i, False)
            project_chunk(C_L0, F=0)
            with pe.Fori(0, 2) as i:
                project_chunk(i + (C_L0 + 1))

            def pair0(i, pace, tiles=()):
                steps = attention_pe(pe, L0, i, tiles)
                project_chunk(i * 2 + C_L0I, stepper(steps, pace))
                finish(steps)
                ada_chunk(i * 2 + (C_L0I + 1), i + 8, False)

            with pe.Fori(0, 4) as i:
                pair0(i, pace0)
            with pe.Fori(4, 7) as i:
                pair0(i, pace0s, [i - 4])
                pe.wait_ge(sp_free, i * 2 - 6)
            pair0(7, pace0t, [3, 4])
            ada_chunk(C_O0, 16, True)
            pe.wait_ge(sp_free, 10)
            pe.wait_ge(S[0].t_free, 8 * L0.n_bank + 1)
            project_chunk(C_O0 + 1, F=1)
            with pe.Fori(1, 4) as j:
                ada_chunk(j * 2 + C_O0, j + 16, True)
                project_chunk(j * 2 + (C_O0 + 1))
            project_chunk(C_L1, F=2)
            with pe.Fori(1, 3) as i:
                project_chunk(i + C_L1)
            with pe.Fori(0, 3) as g:
                steps = chain(attention_pe(pe, L1, g * 4 + x) for x in range(4))
                for n in range(3):
                    project_chunk(g * 3 + (C_L1 + 3 + n), stepper(steps, pace1, n))
                finish(steps)
            with pe.Fori(0, 4) as j:
                steps = attention_pe(pe, L1, j + 12)
                project_chunk(j + (C_L1 + 12), stepper(steps, pace1g))
                finish(steps)
            ada_chunk(C_O1, 20, True)
            pe.wait_ge(S[1].t_free, 16 * L1.n_bank + 1)
            project_chunk(C_O1 + 1, F=3)
            with pe.Fori(1, 4) as j:
                ada_chunk(j * 2 + C_O1, j + 20, True)
                project_chunk(j * 2 + (C_O1 + 1))

        def attention_act(act, L, h, tiles=()):
            s = S[L.n]
            NT, NS = L.n_turn, L.n_scores

            def turn(r, pieces):
                act.wait_ge(s.t_ready, h * NT + (r + 1))
                for (c0, c1), dst in pieces:
                    last = nc.scalar.copy(dst, ps[:, TURN, c0:c1])
                last.then_inc(s.t_hi, 1)

            def scores(n, u, src, width):
                m = n % L.maps
                if m == 0 and L.maps == 2:
                    act.wait_ge(s.w_ready, h * 5 + (u + 1))
                act.wait_ge(s.s_max, h * NS + (n + 1))
                dst = weights[:, m if L.maps == 2 else u, :] if L.maps == 2 or u < TS else wts_p
                dst = dst[:, 0:width]
                nc.scalar.activation(dst if src.ndim == 2 else dst.rearrange("p (b w) -> p b w", b=2),
                                     src, ACT.Exp, bias=small[:, 20 + m:21 + m], scale=L.scale,
                                     accum_out=sums[:, n:n + 1]).then_inc(s.s_exp, 1)

            flat = "p k q -> p (k q)"
            w_pieces = [[((0, 512), wT[0][:, 0:2, :].rearrange(flat))], [((0, 512), wT[0][:, 2:4, :].rearrange(flat))],
                        [((0, 256), wT[0][:, 4, :])]]
            pieces = ([[((0, 512), qT[0][:, 0:512])], [((0, 512), kT[0][:, 0:512])],
                       [((0, 128), qT[0][:, 512:640]), ((128, 384), kT[0][:, 512:768])]]
                      + w_pieces + w_pieces + [[((0, P), wT[0][:, 0, 0:P])]])
            r = n = p = 0
            for kind in L.order:
                if kind == "T":
                    if r == 3:
                        act.wait_ge(s.v_in, h * 32 + 32)
                        nc.scalar.copy(vv[0][:, 0:TT, :], v_in[:, :, :])
                        nc.scalar.copy(vv[0][:, TT, :], cv_in[:, :]).then_inc(s.v_hi, 1)
                    turn(r, pieces[r])
                    r += 1
                elif kind == "S":
                    if n < TS * L.maps:
                        scores(n, n // L.maps, ps[:, SC:SC + 2, 0:320], 640)
                    else:
                        scores(n, TS, ps[:, SC, 0:P], P)
                    n += 1
                elif kind == "P":
                    width = 256 if p < 2 else P
                    act.wait_ge(s.pv_ready, h * 3 + (p + 1))
                    nc.scalar.copy(oT[:, 0:width], ps[:, TURN, 0:width]).then_inc(s.pv_copied, 1)
                    p += 1
                yield

        @block.scalar
        def _(act):
            def split_hi(c, kt):
                i = kt // 2
                act.wait_ge(w_landed[i % RAW], c * 16 * (UNITS // RAW) + 16 * (i // RAW + 1))
                wait_slot_used(act, c, kt)
                nc.scalar.copy(w_hi[:, kt % RING, :], w_raw[:, i % RAW, kt % 2, :]).then_inc(w_hi_ready, 1)

            def split_chunk(c, beside=None, last=False):
                for kt in range(KT):
                    k = kt + AHEAD
                    if k < KT:
                        split_hi(c, k)
                    elif not last:
                        split_hi(c + 1, k - KT)
                    if beside is not None:
                        beside(kt)

            def evacuate(c, n):
                act.wait_ge(stage_free, n + 1)
                for t in range(TT):
                    act.wait_ge(acc_ready, c * 5 + (t + 1 + ACC_CREDIT))
                    nc.scalar.copy(stage[:, t, :], ps[:, t, :]).then_inc(acc_free, 1)
                act.drain().then_inc(stage_full, 1)

            def evacuate_gate(c, n):
                act.wait_ge(stage_free, n + 1)
                for t in range(TT):
                    act.wait_ge(acc_ready, c * 5 + (t + 1 + ACC_CREDIT))
                    nc.scalar.activation(stage[:, t, :], ps[:, t, :], ACT.Tanh, scale=0.5).then_inc(tanh_done, 1)

            def feed_hi(F, kt):
                if F % 2 == 0:
                    act.wait_ge(turn_mid, 8 * F + kt + 1)
                    src = h5
                else:
                    act.wait_ge(turn_ready, 16 * F + kt + 1)
                    src = turned
                nc.scalar.copy(hT_hi[:, kt, :], src).then_inc(turn_hi, 1)

            def feed_beside(F):
                return lambda kt: feed_hi(F, kt + FEED) if kt + FEED < KT else None

            def square_tile(n, m):
                act.drain()
                act.wait_ge(out_done, n * TT + m + 1)
                nc.scalar.activation(junk, stage[:, m, :], ACT.Square,
                                     accum_out=ssq[:, bass.ds((n % 4) * TT + m, 1)]).then_inc(sq_done, 1)

            def stepper(steps, pace, n=0):
                def beside(kt):
                    for _ in range(pace.due_in(n, kt)):
                        next(steps, None)
                return beside

            def finish(steps):
                for _ in steps:
                    pass

            act.wait_ge(setup_pe, 1)
            nc.scalar.copy(vcol[:, :], ps[:, 7, 0:P])
            nc.scalar.copy(bsT[:, :], ps[:, 7, P:P + 8])
            nc.scalar.copy(ws_t[:, :], ps[:, 5:7, :].rearrange("p a b -> p (a b)"))
            act.drain().then_inc(setup_act, 1)
            nc.scalar.activation(small[:, 64:96], vcol[:, 0:32], ACT.Tanh, scale=0.5).then_inc(setup_act, 1)
            act.wait_ge(setup_dve, 2)
            nc.scalar.activation(small[:, 10:12], small[:, 8:10], ACT.Exp).then_inc(setup_act, 1)
            act.sem_inc(S[0].s_exp, 1)
            act.sem_inc(S[1].s_exp, 1)
            for kt in range(AHEAD):
                split_hi(0, kt)

            def square_x(t):
                act.drain()
                act.wait_ge(xt_in, t * 16 + 16)
                nc.scalar.activation(sp_buf[:, :], area[:, 2, :], ACT.Square,
                                     accum_out=ssq[:, bass.ds(t, 1)]).then_inc(sq_done, 1)

            with act.Fori(0, 5) as i:
                split_chunk(i)
                square_x(i)
            with act.Fori(5, 8) as i:
                split_chunk(i)
            for kt in range(FEED):
                feed_hi(0, kt)
            split_chunk(C_L0, feed_beside(0))
            evacuate(C_L0, 0)
            with act.Fori(0, 2) as i:
                split_chunk(i + (C_L0 + 1))
                evacuate(i + (C_L0 + 1), i + 1)

            def pair0(i, pace, evac, tiles=()):
                steps = attention_act(act, L0, i, tiles)
                split_chunk(i * 2 + C_L0I, stepper(steps, pace))
                finish(steps)
                evac(i * 2 + C_L0I, i + 3)
                split_chunk(i * 2 + (C_L0I + 1))

            with act.Fori(0, 4) as i:
                pair0(i, pace0, evacuate)
            with act.Fori(4, 7) as i:
                pair0(i, pace0s, evacuate_gate)
            pair0(7, pace0t, evacuate_gate)

            def output(first, F, n0, last):
                split_chunk(first)
                for kt in range(FEED):
                    feed_hi(F, kt)
                split_chunk(first + 1, feed_beside(F))

                def output_pair(j, last=False):
                    split_chunk(j * 2 + first)
                    split_chunk(j * 2 + (first + 1),
                                lambda kt: square_tile(j + (n0 - 1), kt - 7) if 7 <= kt < 12 else None, last)
                with act.Fori(1, 3) as j:
                    output_pair(j)
                output_pair(3, last)
                for t in range(TT):
                    square_tile(n0 + 3, t)

            output(C_O0, 1, 0, False)
            for kt in range(FEED):
                feed_hi(2, kt)
            split_chunk(C_L1, feed_beside(2))
            evacuate(C_L1, 15)
            with act.Fori(1, 3) as i:
                split_chunk(i + C_L1)
                evacuate(i + C_L1, i + 15)
            with act.Fori(0, 3) as g:
                steps = chain(attention_act(act, L1, g * 4 + x) for x in range(4))
                for n in range(3):
                    split_chunk(g * 3 + (C_L1 + 3 + n), stepper(steps, pace1, n))
                    if n == 2:
                        finish(steps)
                    evacuate(g * 3 + (C_L1 + 3 + n), g * 3 + (18 + n))
            with act.Fori(0, 4) as j:
                steps = attention_act(act, L1, j + 12)
                split_chunk(j + (C_L1 + 12), stepper(steps, pace1g))
                finish(steps)
                evacuate_gate(j + (C_L1 + 12), j + 27)
            output(C_O1, 3, 4, True)

        def rsqrt_parts(dve, x, r, t):
            nc.vector.tensor_scalar(r.bitcast(I32), x.bitcast(I32), 1, None, ALU.logical_shift_right)
            dve.drain()
            nc.vector.tensor_scalar(r.bitcast(I32), r.bitcast(I32), -1.0, float(0x5F3759DF), ALU.mult, ALU.add)
            for _ in range(3):
                yield
                dve.drain()
                nc.vector.tensor_tensor(t, r, r, ALU.mult)
                dve.drain()
                nc.vector.scalar_tensor_tensor(t, t, -0.5, x, ALU.mult, ALU.mult)
                dve.drain()
                nc.vector.scalar_tensor_tensor(r, t, 1.5, r, ALU.add, ALU.mult)

        def rsqrt(dve, x, r, t):
            for _ in rsqrt_parts(dve, x, r, t):
                pass
            dve.drain()

        def norm_head(dve, h):
            s = S[0]
            dve.drain()
            dve.wait_ge(s.qk_in, h * 48 + 48)
            for n, z in enumerate((q_in, k_in)):
                if n == 1:
                    dve.drain()
                nc.vector.tensor_tensor(squares[0], z[:, :, :], z[:, :, :], ALU.mult)
                dve.drain()
                nc.vector.tensor_reduce(small[:, 40 + 5 * n:45 + 5 * n], squares[0], AX_X, ALU.add)
                yield
            dve.drain()
            nc.vector.tensor_scalar(small[:, 40:50], small[:, 40:50], 1.0 / P, EPS, ALU.mult, ALU.add)
            dve.drain()
            rsqrt(dve, small[:, 40:50], small[:, 50:60], small[:, 30:40])
            yield
            for n, (z, g) in enumerate(((q_in, gq), (k_in, gk))):
                nc.vector.tensor_tensor(z[:, :, :], z[:, :, :],
                                        small[:, 50 + 5 * n:55 + 5 * n].unsqueeze(2).to_broadcast([P, TT, P]), ALU.mult)
                dve.drain()
                last = nc.vector.tensor_tensor(z[:, :, :], z[:, :, :], g[:, :].unsqueeze(1).to_broadcast([P, TT, P]),
                                               ALU.mult)
                if n == 0:
                    yield
            dve.drain().then_inc(s.normed, 1)

        def norm_out(dve):
            x, r, t = small[:, 40:45], small[:, 50:55], small[:, 30:35]
            dve.drain()
            nc.vector.tensor_tensor(squares[1], o_head[:, :, :], o_head[:, :, :], ALU.mult)
            yield
            dve.drain()
            nc.vector.tensor_reduce(x, squares[1], AX_X, ALU.add)
            yield
            dve.drain()
            nc.vector.tensor_scalar(x, x, 1.0 / P, EPS, ALU.mult, ALU.add)
            dve.drain()
            yield from rsqrt_parts(dve, x, r, t)
            dve.drain()
            nc.vector.tensor_tensor(o_head[:, :, :], o_head[:, :, :], r.unsqueeze(2).to_broadcast([P, TT, P]), ALU.mult)
            yield
            dve.drain()
            nc.vector.tensor_tensor(o_head[:, :, :], o_head[:, :, :],
                                    gsub[:, :].unsqueeze(1).to_broadcast([P, TT, P]), ALU.mult)
            dve.drain().then_inc(S[1].o_done, 1)

        def heads_dve(dve, first, count):
            before = None
            for x in range(count):
                yield from attention_dve(dve, L1, first + x, before=before)
                before = norm_out(dve)
            for _ in before:
                yield

        def attention_dve(dve, L, h, tiles=(), last_head=False, before=None):
            s = S[L.n]
            NT, NS = L.n_turn, L.n_scores

            def turn(r, pieces):
                dve.wait_ge(s.t_hi, h * NT + (r + 1))
                for (c0, c1), hi, lo in pieces:
                    last_op = nc.vector.tensor_tensor(lo, ps[:, TURN, c0:c1], hi.bitcast(F32), ALU.subtract)
                last_op.then_inc(s.t_free, 1)

            def scores(n, src):
                m = n % L.maps
                dve.drain()
                dve.wait_ge(s.s_ready, h * NS + (n + 1))
                nc.vector.tensor_reduce(small[:, 22 + m:23 + m], src,
                                        AX_X if src.ndim == 2 else mybir.AxisListType.XY, ALU.max)
                dve.drain()
                nc.vector.tensor_scalar(small[:, 20 + m:21 + m], small[:, 22 + m:23 + m], -L.scale, None,
                                        ALU.mult).then_inc(s.s_max, 1)

            def combine(u):
                width = 640 if u < TS else P
                dst = weights[:, 2 + u % 2, :] if u < TS else wts_p[:, :]
                dve.drain()
                dve.wait_ge(s.s_exp, h * NS + ((u + 1) * L.maps + 1))
                nc.vector.reciprocal(inv_sums[:, 2 * u:2 * u + 2], sums[:, 2 * u:2 * u + 2])
                dve.drain()
                nc.vector.scalar_tensor_tensor(small[:, 26:27], sums[:, 2 * u:2 * u + 1], small[:, 12:13],
                                               inv_sums[:, 2 * u + 1:2 * u + 2], ALU.mult, ALU.mult)
                dve.drain()
                nc.vector.scalar_tensor_tensor(dst, weights[:, 1, 0:width], small[:, 26:27], weights[:, 0, 0:width],
                                               ALU.mult, ALU.add).then_inc(s.w_ready, 1)

            def back(n, t0, count):
                dve.drain()
                if L.maps == 1:
                    dve.wait_ge(s.s_exp, h * NS + (t0 + count + 1))
                    nc.vector.reciprocal(inv_sums[:, t0:t0 + count], sums[:, t0:t0 + count])
                    dve.drain()
                dve.wait_ge(s.b_ready, h * 3 + (n + 1))
                if n == 0:
                    dve.wait_ge(s.o_free, h + 1)
                for k in range(count):
                    at = (t0 + k) * L.maps
                    last_op = nc.vector.tensor_scalar(o_head[:, t0 + k, :], ps[:, TURN, k * P:(k + 1) * P],
                                                      inv_sums[:, at:at + 1], None, ALU.mult)
                last_op.then_inc(s.t_free, 1)

            flat = "p k q -> p (k q)"
            w_pieces = [[((0, 512),) + tuple(w[:, 0:2, :].rearrange(flat) for w in wT)],
                        [((0, 512),) + tuple(w[:, 2:4, :].rearrange(flat) for w in wT)],
                        [((0, 256), wT[0][:, 4, :], wT[1][:, 4, :])]]
            pieces = ([[((0, 512), qT[0][:, 0:512], qT[1][:, 0:512])], [((0, 512), kT[0][:, 0:512], kT[1][:, 0:512])],
                       [((0, 128), qT[0][:, 512:640], qT[1][:, 512:640]),
                        ((128, 384), kT[0][:, 512:768], kT[1][:, 512:768])]]
                      + w_pieces + w_pieces + [[((0, P), wT[0][:, 0, 0:P], wT[1][:, 0, 0:P])]])
            next_norm = norm_head(dve, h + 1) if L.n == 0 and not last_head else iter(())
            r = n = b = u = 0
            for kind in L.order:
                if kind == "T":
                    if r == 3:
                        if L.maps == 2:
                            combine(1)
                            u = 2
                        dve.wait_ge(s.v_hi, h + 1)
                        nc.vector.tensor_tensor(vv[1][:, 0:TT, :], v_in[:, :, :], vv[0][:, 0:TT, :].bitcast(F32),
                                                ALU.subtract)
                        nc.vector.tensor_tensor(vv[1][:, TT, :], cv_in[:, :], vv[0][:, TT, :].bitcast(F32),
                                                ALU.subtract)
                        dve.drain().then_inc(s.v_split, 1)
                    if L.maps == 2 and u == 4 and n == TT * L.maps:
                        combine(4)
                        u = 5
                    turn(r, pieces[r])
                    r += 1
                elif kind == "S":
                    if L.maps == 2 and n % L.maps == 0 and n // L.maps > u:
                        combine(u)
                        u += 1
                    scores(n, ps[:, SC:SC + 2, 0:320] if n < TS * L.maps else ps[:, SC, 0:P])
                    n += 1
                elif kind == "B":
                    back(b, 2 * b, 2 if b < 2 else 1)
                    b += 1
                if r >= 8:
                    next(next_norm, None)
                if before is not None:
                    next(before, None)
                if b == 3 and L.n == 0:
                    for _ in next_norm:
                        pass
                    dve.drain().then_inc(s.o_done, 1)
                yield
            for tile in tiles:
                va = sp_buf[:, 0:1024]
                dve.wait_ge(sp_in, tile * 32 + 32)
                for k in range(2):
                    nc.vector.bn_stats(small[:, 60 + 6 * k:66 + 6 * k], va[:, k * NC:(k + 1) * NC])
                dve.drain()
                nc.vector.bn_aggr(small[:, 72:74], small[:, 60:72])
                dve.drain()
                nc.vector.tensor_scalar(small[:, 74:75], small[:, 73:74], EPS, None, ALU.add)
                dve.drain()
                rsqrt(dve, small[:, 74:75], small[:, 75:76], small[:, 76:77])
                nc.vector.tensor_scalar(va, va, small[:, 72:73], small[:, 75:76], ALU.subtract,
                                        ALU.mult).then_inc(vn_ready, 1)
                yield
                for half in range(2):
                    dve.wait_ge(sp_ready, tile * 2 + half + 1)
                    for g in range(4):
                        y = sp_buf[:, 1024 + (half * 4 + g) * P:1024 + (half * 4 + g + 1) * P]
                        nc.vector.scalar_tensor_tensor(y, ps[:, TURN, g * P:(g + 1) * P],
                                                       bsT[:, half * 4 + g:half * 4 + g + 1], y, ALU.add, ALU.mult)
                    dve.drain().then_inc(sp_free, 1)
                    yield

        @block.vector
        def _(dve):
            def split_lo(c, kt):
                i = kt // 2
                dve.wait_ge(w_hi_ready, c * KT + (kt + 1))
                nc.vector.tensor_tensor(w_lo[:, kt % RING, :], w_raw[:, i % RAW, kt % 2, :],
                                        w_hi[:, kt % RING, :].bitcast(F32), ALU.subtract).then_inc(w_lo_ready, 1)
                if kt % 2 == 1:
                    dve.drain().then_inc(raw_free, 1)

            def split_chunk(c, beside=None, last=False):
                for kt in range(KT):
                    k = kt + AHEAD
                    if k < KT:
                        split_lo(c, k)
                    elif not last:
                        split_lo(c + 1, k - KT)
                    if beside is not None:
                        beside(kt)

            def evacuate_gate(c, n, m):
                for t in range(TT):
                    dve.wait_ge(tanh_done, m * TT + (t + 1))
                    nc.vector.scalar_tensor_tensor(stage[:, t, :], stage[:, t, :], 1.0, ps[:, t, :], ALU.add,
                                                   ALU.mult).then_inc(acc_free, 1)
                dve.drain().then_inc(stage_full, 1)

            def ada_rows(c, n):
                dve.wait_ge(acc_ready, c * 5 + (5 + ACC_CREDIT))
                nc.vector.tensor_copy(modrow[:, :], ps[0:4, 0, :]).then_inc(row_ready, 1)
                dve.wait_ge(mod_ready, n + 1)

            def ada_columns(c, n, l, i):
                ada_rows(c, n)
                nc.vector.tensor_tensor(modcol[l][:, bass.ds(i * 4, 4), :],
                                        ps[:, 1, 0:8].rearrange("p (k c) -> p k c", c=2),
                                        vcol[:, bass.ds(i * 4 + (64 + 32 * l), 4)].unsqueeze(2).to_broadcast([P, 4, 2]),
                                        ALU.add).then_inc(acc_free, 5)

            def ada_gate(c, n, m):
                dve.drain()
                ada_rows(c, n)
                dve.wait_ge(gb_in, m * 16 + 16)
                for k in range(2):
                    nc.vector.tensor_tensor(gate_b[:, k, :], ps[:, 1 + k, :], gate_bias, ALU.add)
                dve.drain().then_inc(gb_free, 1)
                dve.drain().then_inc(acc_free, 5)

            def scale_columns(l):
                dve.drain()
                nc.vector.scalar_tensor_tensor(modcol[l][:, 16:32, :], modcol[l][:, 16:32, :], 1.0,
                                               vcol[:, 32 + 16 * l:48 + 16 * l].unsqueeze(2).to_broadcast([P, 16, 2]),
                                               ALU.add, ALU.mult)
                dve.drain()

            def row_norms(partial):
                dve.drain()
                if partial:
                    nc.vector.tensor_reduce(small[:, 60:65], ssq[:, :].rearrange("p (j t) -> p t j", j=4), AX_X,
                                            ALU.add)
                    dve.drain()
                src = small[:, 60:65] if partial else ssq[:, 0:TT]
                nc.vector.tensor_scalar(small[:, 65:70], src, 1.0 / D, EPS, ALU.mult, ALU.add)
                dve.drain()
                rsqrt(dve, small[:, 65:70], rstd[:, :], small[:, 70:75])

            def feed_block(F, b):
                x = blk[b % 2]
                if F % 2 == 0:
                    dve.wait_ge(x_in[b % 2], F * 32 + (b // 2 + 1) * 32)
                    for t in range(TT):
                        nc.vector.tensor_scalar(x[:, t, :], x[:, t, :], rstd[:, t:t + 1], None, ALU.mult)
                else:
                    dve.wait_ge(o_in[b % 2], F // 2 * 32 + (b // 2 + 1) * 16)
                    dve.wait_ge(g_in, F // 2 * 64 + (b + 1) * 16)
                    nc.vector.scalar_tensor_tensor(x, stage[:, :, :], 0.5, x, ALU.mult, ALU.mult)
                dve.drain().then_inc(src_ready, 1)

            def feed_lo(F, kt):
                src = h5 if F % 2 == 0 else turned
                dve.wait_ge(turn_hi, 16 * F + kt + 1)
                nc.vector.tensor_tensor(hT_lo[:, kt, :], src, hT_hi[:, kt, :].bitcast(F32),
                                        ALU.subtract).then_inc(turn_free, 1)

            def feed_step(F, k):
                if k % 4 == 0 and k < KT:
                    feed_block(F, k // 4)
                if F % 2 == 1:
                    if k < KT:
                        feed_lo(F, k)
                    return
                if k > 0:
                    feed_lo(F, k - 1)
                if k < KT:
                    dve.drain()
                    dve.wait_ge(turn_ready, 16 * F + k + 1)
                    for cond, (c0, c1) in enumerate(((0, TS * P), (TS * P, NTOK))):
                        nc.vector.tensor_scalar(h5[:, c0:c1], turned[:, c0:c1],
                                                modcol[F // 2][:, 16 + k, cond:cond + 1],
                                                modcol[F // 2][:, k, cond:cond + 1], ALU.mult, ALU.add)
                    dve.drain().then_inc(turn_mid, 1)

            def feed_beside(F):
                return lambda kt: feed_step(F, kt + FEED) if kt + FEED <= KT else None

            def stepper(steps, pace, n=0):
                def beside(kt):
                    for _ in range(pace.due_in(n, kt)):
                        next(steps, None)
                return beside

            def finish(steps):
                for _ in steps:
                    pass

            dve.sem_inc(raw_free, RAW)
            dve.sem_inc(acc_free, 5)
            for s in S:
                dve.sem_inc(s.t_free, 1)
                dve.sem_inc(s.w_ready, 1)
            nc.vector.memset(cst[:, :].bitcast(F32), 0.0)
            dve.wait_ge(setup_act, 2)
            nc.vector.scalar_tensor_tensor(small[:, 32:64], small[:, 64:96], 1.0, vcol[:, 0:32], ALU.add, ALU.mult)
            dve.drain()
            nc.vector.tensor_scalar(small[:, 32:64], small[:, 32:64], 0.5, None, ALU.mult)
            dve.drain()
            parts = cst[:, 0:4 * KT].rearrange("p (k q) -> p k q", q=4)
            for k in range(2):
                x = small[:, 32 + 16 * k:48 + 16 * k]
                nc.vector.tensor_copy(parts[:, :, 2 * k], x)
                dve.drain()
                nc.vector.tensor_tensor(parts[:, :, 2 * k + 1], x, parts[:, :, 2 * k].bitcast(F32), ALU.subtract)
            dve.drain().then_inc(setup_dve, 1)
            dve.wait_ge(setup_in, 16 * N_SETUP)
            for k in range(2):
                nc.vector.tensor_tensor(lam4[:, 2 * k, :], lam4[:, 2 * k, :], lam4[:, 2 * k + 1, :], ALU.mult)
            dve.drain()
            nc.vector.tensor_reduce(small[:, 8:10], lam4[:, :, :].rearrange("p (a b) d -> p a b d", b=2)[:, :, 0, :],
                                    AX_X, ALU.add)
            dve.drain().then_inc(setup_dve, 1)
            dve.wait_ge(setup_act, 3)
            nc.vector.tensor_tensor(small[:, 12:13], small[:, 11:12], small[:, 10:11], ALU.subtract)
            dve.drain()
            nc.vector.tensor_scalar(small[:, 12:13], small[:, 12:13], -LAMBDA_INIT, None, ALU.add)
            nc.vector.tensor_scalar(gsub[:, :], gsub[:, :], 1.0 - LAMBDA_INIT, None, ALU.mult)
            for kt in range(AHEAD):
                split_lo(0, kt)
            with dve.Fori(0, 8) as i:
                split_chunk(i)
                ada_columns(i, i, 0, i)
            scale_columns(0)
            dve.wait_ge(sq_done, 5)
            row_norms(partial=False)
            for k in range(FEED):
                feed_step(0, k)
            split_chunk(C_L0, feed_beside(0))
            split_chunk(C_L0 + 1)
            first_norm = norm_head(dve, 0)
            split_chunk(C_L0 + 2, lambda kt: next(first_norm, None) if 4 <= kt < 9 else None)

            def pair0(i, pace, gate=False, tiles=(), last_head=False):
                steps = attention_dve(dve, L0, i, tiles, last_head)
                split_chunk(i * 2 + C_L0I, stepper(steps, pace))
                finish(steps)
                if gate:
                    evacuate_gate(i * 2 + C_L0I, i + 3, i - 4)
                split_chunk(i * 2 + (C_L0I + 1))
                ada_columns(i * 2 + (C_L0I + 1), i + 8, 1, i)

            with dve.Fori(0, 4) as i:
                pair0(i, pace0)
            with dve.Fori(4, 7) as i:
                pair0(i, pace0s, True, [i - 4])
            pair0(7, pace0t, True, [3, 4], last_head=True)
            scale_columns(1)

            def multiply(c, t):
                dve.wait_ge(acc_ready, c * 5 + (t + 1 + ACC_CREDIT))
                nc.vector.tensor_tensor(stage[:, t, :], ps[:, t, :], gate_b[:, t // TS, :],
                                        ALU.mult).then_inc(acc_free, 1)

            def add_old(n, t):
                if t == 0:
                    dve.drain()
                    dve.wait_ge(xo_in, n * 32 + 32)
                nc.vector.tensor_tensor(stage[:, t, :], stage[:, t, :], x_old[:, t, :], ALU.add).then_inc(out_done, 1)
                if t == TT - 1:
                    dve.drain().then_inc(xo_free, 1)
                    dve.drain().then_inc(stage_full, 1)

            def output(first, F, n0, m0, last):
                split_chunk(first)
                dve.wait_ge(S[F // 2].o_free, (8 if F == 1 else 16) + 1)
                ada_gate(first, m0, n0)
                for k in range(FEED):
                    feed_step(F, k)
                split_chunk(first + 1, feed_beside(F))
                dve.drain()
                for t in range(TT):
                    multiply(first + 1, t)

                def output_pair(j, last=False):
                    split_chunk(j * 2 + first)
                    ada_gate(j * 2 + first, j + m0, j + n0)
                    split_chunk(j * 2 + (first + 1),
                                lambda kt: add_old(j + (n0 - 1), kt - 1) if 1 <= kt < 6 else None, last)
                    dve.drain()
                    dve.wait_ge(stage_free, j + (11 if F == 1 else 31) + 1)
                    dve.wait_ge(sq_done, j * TT + (n0 * TT + TT))
                with dve.Fori(1, 3) as j:
                    output_pair(j)
                    for t in range(TT):
                        multiply(j * 2 + (first + 1), t)
                output_pair(3, last)
                dve.wait_ge(xo_in, (n0 + 3) * 32 + 32)
                for t in range(TT + 1):
                    if t < TT:
                        multiply(first + 7, t)
                    dve.drain()
                    if t > 0:
                        add_old(n0 + 3, t - 1)
                dve.wait_ge(sq_done, TT + (n0 + 4) * TT)
                row_norms(partial=True)

            output(C_O0, 1, 0, 16, False)
            for k in range(FEED):
                feed_step(2, k)
            split_chunk(C_L1, feed_beside(2))
            with dve.Fori(1, 3) as i:
                split_chunk(i + C_L1)
            with dve.Fori(0, 3) as g:
                steps = heads_dve(dve, g * 4, 4)
                for n in range(3):
                    split_chunk(g * 3 + (C_L1 + 3 + n), stepper(steps, pace1, n))
                finish(steps)
            with dve.Fori(0, 4) as j:
                steps = heads_dve(dve, j + 12, 1)
                split_chunk(j + (C_L1 + 12), stepper(steps, pace1g))
                finish(steps)
                evacuate_gate(j + (C_L1 + 12), j + 27, j + 4)
            output(C_O1, 3, 4, 20, True)
            dve.wait_ge(fg_in, 16)
            for t in range(TT):
                dve.wait_ge(fin_in[t % 2], (t // 2 + 1) * 16)
                nc.vector.scalar_tensor_tensor(area[:, t % 2, :], area[:, t % 2, :], rstd[:, t:t + 1], area[:, 2, :],
                                               ALU.mult, ALU.mult).then_inc(fin_ready, 1)

        @block.gpsimd
        def _(pool):
            def wait(s, value):
                pool.wait_ge(s, value)
                pool.sem_inc(pool_passed, 1)

            def z_at(l, i):
                return z_d[l][i] if isinstance(i, int) else z_d[l][bass.ds(i, 1)].squeeze(0)

            def load_qk(L, h):
                s = S[L.n]
                z = z_d[L.n]
                if L.n == 0:
                    q = z_at(0, h // 4 + 1)[:, :, bass.ds((h % 4) * P, P)]
                    k = z[0, :, :, bass.ds(h // 4 * P, P)]
                    ck = a["cache_k0"][0].rearrange("t h d -> t (h d)")[:, bass.ds(h // 4 * P, P)]
                else:
                    q, k = (z_at(1, h // 4 * 3 + n)[:, :, bass.ds((h % 4) * P, P)] for n in range(2))
                    ck = a["cache_k1"][0].rearrange("t h m d -> t (h m d)")[:, bass.ds(h * P, P)]
                for dst, src in ((q_in[:, :, :], q), (k_in[:, :, :], k), (ck_in[:, :], ck)):
                    pool.dma_start(dst, src).then_inc(s.qk_in, 16)

            def load_v(L, h):
                s = S[L.n]
                if L.n == 0:
                    v = z_d[0][0, :, :, bass.ds(h // 4 * P + 256, P)]
                    cv = a["cache_v0"][0].rearrange("t h d -> t (h d)")[:, bass.ds(h // 4 * P, P)]
                else:
                    v = z_at(1, h // 4 * 3 + 2)[:, :, bass.ds((h % 4) * P, P)]
                    cv = a["cache_v1"][0].rearrange("t h d -> t (h d)")[:, bass.ds(h * P, P)]
                for dst, src in ((v_in[:, :, :], v), (cv_in[:, :], cv)):
                    pool.dma_start(dst, src).then_inc(s.v_in, 16)

            def rotate_head(L, h):
                s = S[L.n]
                if L.n == 0:
                    wait(s.normed, h + 1)
                else:
                    wait(s.qk_in, h * 48 + 48)
                half = L.dk // 4
                halves = "p (x s j) -> p x s j"
                for z in (q_in, k_in):
                    flat = z[:, 0:TS, :].rearrange("p t d -> p (t d)")
                    nc.gpsimd.tensor_tensor(rope_a[:, :], flat, rope_c[:, :], ALU.mult)
                    z4 = flat.rearrange(halves, s=2, j=half)
                    b4 = rope_b[:, :].rearrange(halves, s=2, j=half)
                    s4 = rope_s[:, :].rearrange(halves, s=2, j=half)
                    for k in range(2):
                        nc.gpsimd.tensor_tensor(b4[:, :, k, :], z4[:, :, 1 - k, :], s4[:, :, k, :], ALU.mult)
                    pool.drain()
                    nc.gpsimd.tensor_tensor(flat, rope_a[:, :], rope_b[:, :], ALU.add)
                    pool.drain()
                pool.drain().then_inc(s.roped, 1)
                if L.n == 0:
                    pool.dma_start(kn_d[h] if isinstance(h, int) else kn_d[bass.ds(h, 1)].squeeze(0),
                                   k_in[:, TS, :]).then_inc(kn_stored, 16)

            def next_qk(L, h):
                wait(S[L.n].t_ready, h * L.n_turn + (3 - L.n_turn))
                if L.n == 0:
                    wait(kn_stored, h * 16)
                load_qk(L, h)

            def next_v(L, h):
                wait(S[L.n].v_split, h)
                load_v(L, h)

            def store_head(L, h):
                wait(S[L.n].o_done, h + 1)
                at = h * P + (1024 if L.n == 0 else 0)
                pool.dma_start(o_d[L.n].rearrange("t p n -> p t n")[:, :, bass.ds(at, P)],
                               o_head[:, :, :]).then_inc(S[L.n].o_stored, 16)

            def free_head(L, h):
                wait(S[L.n].o_stored, h * 16 + 16)
                pool.sem_inc(S[L.n].o_free, 1)

            def store_stage(n, dst):
                wait(stage_full, n + 1)
                pool.dma_start(dst, stage[:, :, :]).then_inc(stage_stored, 16)

            def free_stage(n):
                wait(stage_stored, n * 16 + 16)
                pool.sem_inc(stage_free, 1)

            def load_spatial(t):
                for n in range(4):
                    idx = (5, 6, 3, 4)[n]
                    if n % 2 == 0:
                        z = z_d[0].rearrange("i p t n -> t p i n")
                        z = z[t] if isinstance(t, int) else z[bass.ds(t, 1)].squeeze(0)
                        pool.dma_start(sp_buf[:, n * NC:(n + 2) * NC].rearrange("p (i n) -> p i n", i=2),
                                       z[:, idx:idx + 2, :]).then_inc(sp_in, 16)

            def store_spatial(t):
                wait(sp_free, t * 2 + 2)
                o = o_d[0][t] if isinstance(t, int) else o_d[0][bass.ds(t, 1)].squeeze(0)
                pool.dma_start(o[:, 0:1024], sp_buf[:, 1024:2048]).then_inc(sp_stored, 16)

            pool.sem_inc(stage_free, 1)
            for s in S:
                pool.sem_inc(s.o_free, 1)
            xs = a["x_sample"][0].rearrange("(t p) d -> t p d", p=P)
            pool.dma_start(area[:, 2, :], xs[0]).then_inc(xt_in, 16)
            for t in range(1, TT):
                wait(sq_done, t)
                pool.dma_start(area[:, 2, :], xs[t] if t < TS else a["x_prompt"][0]).then_inc(xt_in, 16)
            wait(sq_done, 5)

            def load_x(b, sample, prompt):
                cols = slice(b * NC, (b + 1) * NC)
                pool.dma_start(blk[b % 2][:, 0:TS, :], sample[:, :, cols]).then_inc(x_in[b % 2], 16)
                pool.dma_start(blk[b % 2][:, TS, :], prompt[:, cols]).then_inc(x_in[b % 2], 16)

            def feed_x(F, sample, prompt):
                for b in range(4):
                    if b >= 2:
                        wait(turn_ready, 16 * F + 4 * (b - 1))
                    load_x(b, sample, prompt)

            x0 = (xs.rearrange("t p d -> p t d"), a["x_prompt"][0])
            feed_x(0, *x0)
            store_stage(0, z_at(0, 0))
            free_stage(0)
            store_stage(1, z_at(0, 1))
            free_stage(1)
            load_qk(L0, 0)
            load_v(L0, 0)
            rotate_head(L0, 0)
            store_stage(2, z_at(0, 2))
            free_stage(2)

            def pair0(i, tiles=(), hold=False):
                if tiles:
                    load_spatial(tiles[0])
                next_qk(L0, i + 1)
                next_v(L0, i + 1)
                rotate_head(L0, i + 1)
                store_head(L0, i)
                free_head(L0, i)
                if tiles:
                    store_spatial(tiles[0])
                    wait(sp_stored, tiles[0] * 16 + 16)
                    pool.sem_inc(stage_free, 1)
                store_stage(i + 3, z_at(0, i + 3))
                if hold:
                    wait(stage_stored, (i + 3) * 16 + 16)
                else:
                    free_stage(i + 3)

            with pool.Fori(0, 3) as i:
                pair0(i)
            pair0(3, hold=True)
            with pool.Fori(4, 7) as i:
                pair0(i, [i - 4], hold=True)

            def load_bias(l, j):
                pool.dma_start(gate_bias, a[f"b_ada{l}"][bass.ds(j * NC + 2 * D, NC)].unsqueeze(0)
                               .to_broadcast([P, NC])).then_inc(gb_in, 16)

            def load_y(l, b):
                pool.dma_start(blk[b % 2], o_d[l].rearrange("t p n -> p t n")[:, :, b * NC:(b + 1) * NC]).then_inc(
                    o_in[b % 2], 16)

            def load_g(l, b):
                pool.dma_start(stage[:, :, :], z_d[l][b + (7 if l == 0 else 12)]).then_inc(g_in, 16)

            def load_old(src, j):
                col = bass.ds(j * NC, NC)
                pool.dma_start(x_old[:, 0:TS, :], src[0][:, :, col]).then_inc(xo_in, 16)
                pool.dma_start(x_old[:, TS, :], src[1][:, col]).then_inc(xo_in, 16)

            load_spatial(3)
            load_bias(0, 0)
            store_head(L0, 7)
            free_head(L0, 7)
            store_spatial(3)
            wait(sp_stored, 64)
            load_spatial(4)
            store_spatial(4)
            wait(sp_stored, 80)
            pool.sem_inc(stage_free, 1)
            store_stage(10, z_at(0, 10))
            load_y(0, 0)
            load_y(0, 1)
            free_stage(10)
            load_g(0, 0)

            def feed_y(l, F):
                for b in range(1, 4):
                    wait(src_ready, 4 * F + b)
                    load_g(l, b)
                    if b >= 2:
                        wait(turn_ready, 16 * F + 4 * (b - 1))
                        load_y(l, b)
                wait(turn_ready, 16 * F + 12)

            wait(kn_stored, 16 * 8)
            for t, n in ((rope_c, 0), (rope_s, 1)):
                pool.dma_start(t[:, :], a["rope"][1, n]).then_inc(copied, 16)
            for g in range(2):
                pool.dma_start(new_k0[0][:, g, :], kn_d[4 * g]).then_inc(copied, 16)
            pool.dma_start(new_v0[0].rearrange("t h d -> t (h d)"), z_d[0][0, :, TS, 256:512]).then_inc(copied, 16)

            def output(l, F, n0, s0, src, dst):
                feed_y(l, F)
                load_old(src, 0)
                wait(gb_free, n0 + 1)
                load_bias(l, 1)
                dst = dst.rearrange("t p d -> p t d")

                def output_chunk(j, bias):
                    wait(xo_free, j + (n0 + 1))
                    load_old(src, j + 1)
                    store_stage(j + s0, dst[:, :, bass.ds(j * NC, NC)])
                    if bias:
                        wait(gb_free, j + (n0 + 2))
                        load_bias(l, j + 2)
                    free_stage(j + s0)

                with pool.Fori(0, 2) as j:
                    output_chunk(j, True)
                output_chunk(2, False)
                wait(xo_free, n0 + 4)
                store_stage(s0 + 3, dst[:, :, 3 * NC:4 * NC])

            output(0, 1, 0, 11, x0, x_d)
            x1 = (x_d.rearrange("t p d -> p t d")[:, 0:TS, :], x_d[TS])
            load_x(0, *x1)
            load_x(1, *x1)
            free_stage(14)
            for b in (2, 3):
                wait(turn_ready, 32 + 4 * (b - 1))
                load_x(b, *x1)
            wait(copied, 16 * 5)
            for n in range(2):
                store_stage(15 + n, z_at(1, n))
                free_stage(15 + n)
            load_qk(L1, 0)
            rotate_head(L1, 0)
            store_stage(17, z_at(1, 2))
            free_stage(17)
            load_v(L1, 0)
            with pool.Fori(0, 3) as g:
                for x in range(4):
                    h = g * 4 + x
                    next_qk(L1, h + 1)
                    rotate_head(L1, h + 1)
                    if x == 1:
                        store_stage(g * 3 + 18, z_at(1, g * 3 + 3))
                    if x < 3:
                        next_v(L1, h + 1)
                    if x == 2:
                        store_stage(g * 3 + 19, z_at(1, g * 3 + 4))
                    store_head(L1, h)
                    if x == 3:
                        store_stage(g * 3 + 20, z_at(1, g * 3 + 5))
                    if x > 0:
                        free_stage(g * 3 + (17 + x))
                    free_head(L1, h)
                next_v(L1, g * 4 + 4)
            with pool.Fori(0, 3) as j:
                next_qk(L1, j + 13)
                rotate_head(L1, j + 13)
                next_v(L1, j + 13)
                store_head(L1, j + 12)
                free_head(L1, j + 12)
                store_stage(j + 27, z_at(1, j + 12))
                free_stage(j + 27)
            wait(gb_free, 4)
            load_bias(1, 0)
            store_head(L1, 15)
            free_head(L1, 15)
            load_y(1, 0)
            load_y(1, 1)
            store_stage(30, z_at(1, 15))
            free_stage(30)
            load_g(1, 0)
            for g in range(4):
                heads = slice(4 * g, 4 * g + 4)
                pool.dma_start(new_k1[0][:, heads].rearrange("t h m d -> t (h m d)"),
                               z_d[1][3 * g + 1, :, TS, :]).then_inc(copied, 16)
                pool.dma_start(new_v1[0][:, heads].rearrange("t h d -> t (h d)"),
                               z_d[1][3 * g + 2, :, TS, :]).then_inc(copied, 16)
            output(1, 3, 4, 31, x1, x2_d)
            free_stage(34)
            pool.dma_start(area[:, 2, :], a["final_g"].unsqueeze(0).to_broadcast([P, D])).then_inc(fg_in, 16)
            ys = y_sample[0].rearrange("(t p) d -> t p d", p=P)
            for t in range(TT + 2):
                if t >= 2:
                    wait(fin_ready, t - 1)
                    pool.dma_start(ys[t - 2] if t - 2 < TS else y_prompt[0], area[:, t % 2, :]).then_inc(fin_stored, 16)
                if t < TT:
                    if t >= 2:
                        wait(fin_stored, (t - 1) * 16)
                    pool.dma_start(area[:, t % 2, :], x2_d[t]).then_inc(fin_in[t % 2], 16)
            wait(fin_stored, 80)
            wait(copied, 16 * 13)


def shape_constants():
    import numpy as np
    layout = np.zeros((P, 386), np.float32)
    layout[:, 0:128] = np.eye(P, dtype=np.float32)
    layout[0:2, 128:256] = 1.0
    layout[2:4, 256:384] = 1.0
    layout[0:2, 384] = 1.0
    layout[2:4, 385] = 1.0
    rope = np.zeros((2, 2, P, TS * P), np.float32)
    tok = np.arange(TS * P)
    pos = [(tok // 64).astype(np.float32), (tok % 64).astype(np.float32)]
    for l, dk in enumerate((128, 64)):
        half = dk // 4
        freqs = np.float32(10000.0) ** (-np.arange(half, dtype=np.float32) / np.float32(half))
        cols = []
        for axis in range(2):
            ang = pos[axis][:, None] * freqs[None, :]
            cols.append((np.cos(ang), np.sin(ang)))
        c = np.concatenate([np.concatenate([x, x], 1) for x, _ in cols], 1)
        s = np.concatenate([np.concatenate([-x, x], 1) for _, x in cols], 1)
        for n, tab in enumerate((c, s)):
            tab = np.tile(tab, (1, P // dk)).astype(np.float32)
            rope[l, n] = tab.reshape(TS, P, P).transpose(1, 0, 2).reshape(P, TS * P)
    return {"layout": layout, "rope": rope}


_INS = ["x_prompt", "x_sample", "cache_k0", "cache_v0", "cache_k1", "cache_v1", "c", "c_ctx",
        "w_ada0", "b_ada0", "norm_g0", "w_in0", "w_s0", "b_s0", "q_norm_g0", "k_norm_g0", "w_out0",
        "w_ada1", "b_ada1", "norm_g1", "w_in1", "lambda_q1", "lambda_k1", "lambda_q2", "lambda_k2",
        "subln_g1", "w_out1", "final_g"]
_OUTS = [(1, 128, 2048), (1, 512, 2048), (1, 128, 2, 128), (1, 128, 2, 128), (1, 128, 16, 2, 64), (1, 128, 16, 128)]


def kernel(**inputs):
    import numpy as _np
    import concourse.bacc as _bacc
    from concourse import mybir as _mybir
    from concourse.bass_utils import run_bass_kernel_spmd as _run

    nc = _bacc.Bacc("TRN2", target_bir_lowering=False, num_devices=1)
    arrays, a = {}, {}
    given = {name: _np.ascontiguousarray(inputs[name]) for name in _INS}
    for name, x in {**given, **shape_constants()}.items():
        arrays[f"in_{name}_dram"] = x
        a[name] = nc.dram_tensor(f"in_{name}_dram", x.shape, _mybir.dt.from_np(x.dtype), kind="ExternalInput").ap()
    outs = [nc.dram_tensor(f"out_{i}_dram", shape, _mybir.dt.float32, kind="ExternalOutput").ap()
            for i, shape in enumerate(_OUTS)]
    kernel_program(nc, a, outs)
    r = _run(nc, [arrays], core_ids=[0])
    return tuple(r.results[0][f"out_{i}_dram"] for i in range(len(_OUTS)))
```

```python
import math
from contextlib import ExitStack

import concourse.bass as bass
from concourse import mybir

F32 = mybir.dt.float32
F32R = mybir.dt.float32r
I32 = mybir.dt.int32
ACT = mybir.ActivationFunctionType
ALU = mybir.AluOpType
AX_X = mybir.AxisListType.X

P = 128
D = 2048
KT = D // P
NC = 512
TS, TT = 4, 5
NTOK = TT * P
EPS = 1e-6
UNITS = KT // 2
RAW = 8
RING = 4
AHEAD = 2
FEED = 3
W_CREDIT = RING
ACC_CREDIT = 1
N_SETUP = 6 + 3 + 3 + 4 + 2
LAMBDA_INIT = 0.8 - 0.6 * math.exp(-0.3)

C_ADA0 = 0
C_L0 = 8
C_L0I = 11
C_O0 = 27
C_L1 = 35
C_O1 = 51
C_END = 59

SLOTS = KT * TT

ORDER0 = ["T", "T", "T", "S", "S", "T", "S", "T", "T", "S", "P", "S", "B", "T", "T", "T", "P", "B", "T", "P", "B"]
ORDER1 = ["T", "T", "T", "S", "S", "S", "S", "T", "S", "T", "S", "T", "S", "P", "S", "B", "S", "T", "S",
          "T", "T", "P", "B", "T", "P", "B"]
ORDER0S = ["T", "T", "T", "S", "S", "T", "S", "T", "T", "S", "P", "S", "B", "L", "T", "T", "T", "P", "B", "G", "G",
           "T", "P", "B"]
ORDER0T = ["T", "T", "T", "S", "S", "T", "S", "T", "T", "S", "P", "S", "B", "L", "T", "T", "T", "G", "G", "L", "P",
           "B", "G", "G", "T", "P", "B"]
AT0 = [0, 3, 6, 10, 14, 18, 20, 24, 28, 31, 34, 37, 41, 43, 46, 49, 53, 56, 58, 62, 65]
AT0S = [0, 2, 4, 7, 11, 15, 18, 20, 23, 25, 28, 30, 32, 34, 40, 42, 44, 47, 49, 52, 55, 58, 62, 65]
AT0T = [0, 2, 4, 7, 11, 15, 18, 20, 23, 25, 28, 30, 32, 34, 39, 41, 43, 46, 48, 49, 52, 54, 58, 61, 63, 67, 70]
AT1 = [0, 2, 4, 7, 10, 14, 18, 24, 26, 28, 31, 32, 35, 36, 40, 41, 44, 45, 48, 49, 51, 52, 54, 56, 58, 59]


class Layer:

    def __init__(self, n, heads, maps, order):
        self.order = order
        self.n, self.heads, self.maps = n, heads, maps
        self.dk = P // maps
        self.scale = self.dk ** -0.5
        self.n_scores = maps * TT
        self.n_turn = 10
        self.n_bank = 13


def chain(parts):
    for part in parts:
        yield from part


def kernel_program(nc, a, outs):
    L0, L1 = Layer(0, 8, 1, ORDER0), Layer(1, 16, 2, ORDER1)
    y_prompt, y_sample, new_k0, new_v0, new_k1, new_v1 = outs

    ctx = ExitStack()
    with ctx:
        def sb(name, shape, dt=F32):
            return ctx.enter_context(nc.sbuf_tensor(name, shape, dt))

        def sem(name):
            return ctx.enter_context(nc.semaphore(name))

        hT_hi = sb("hT_hi", [P, KT, NTOK], F32R)
        hT_lo = sb("hT_lo", [P, KT, NTOK], F32R)
        w_raw = sb("w_raw", [P, RAW, 2, NC])
        w_hi = sb("w_hi", [P, RING, NC], F32R)
        w_lo = sb("w_lo", [P, RING, NC], F32R)
        stage = sb("stage", [P, TT, NC])
        rope_c = sb("rope_c", [P, TS * P])
        rope_s = sb("rope_s", [P, TS * P])
        consts = sb("consts", [P, 386])
        ident = consts[:, 0:128]
        sel_row = [consts[0:4, 128:256], consts[0:4, 256:384]]
        sel_col = consts[0:4, 384:386]
        vcol = sb("vcol", [P, P])
        cst = sb("cst", [P, KT * 4 + P], F32R)
        modrow = sb("modrow", [4, NC])
        modcol = [sb(f"modcol{l}", [P, 32, 2]) for l in range(2)]
        gq = sb("gq", [P, P])
        gk = sb("gk", [P, P])
        gsub = sb("gsub", [P, P])
        bsT = sb("bsT", [P, 8])
        small = sb("small", [P, 96])
        work = sb("work", [P, 3 * D])
        taken = [0]

        def part(*shape):
            n = math.prod(shape)
            at = work[:, taken[0]:taken[0] + n]
            taken[0] += n
            return at if len(shape) == 1 else at.rearrange("p (a b) -> p a b", b=shape[1])

        q_in = part(TT, P)
        k_in = part(TT, P)
        v_in = part(TT, P)
        ck_in = part(P)
        cv_in = part(P)
        rope_b = part(TS * P)
        weights = part(4, 640)
        o_head = part(TT, P)
        area = work[:, :].rearrange("p (a n) -> p a n", a=3)
        lam4 = area[:, 1, 1024:1280].rearrange("p (n d) -> p n d", n=4)
        rope_a = sb("rope_a", [P, TS * P])
        qT = [sb("qT_hi", [P, NTOK], F32R), sb("qT_lo", [P, NTOK], F32R)]
        kT = [sb("kT_hi", [P, NTOK + P], F32R), sb("kT_lo", [P, NTOK + P], F32R)]
        vv = [sb("v_hi", [P, TT + 1, P], F32R), sb("v_lo", [P, TT + 1, P], F32R)]
        wT = [sb("wT_hi", [P, 5, 256], F32R), sb("wT_lo", [P, 5, 256], F32R)]
        oT = sb("oT", [P, 256])

        blk = [work[:, n * TT * NC:(n + 1) * TT * NC].rearrange("p (t n) -> p t n", t=TT) for n in range(2)]
        raw = w_raw[:, :, :, :].rearrange("p i k n -> p (i k n)")
        last_g = raw[:, 0:D]
        last_x = [raw[:, D:D + TT * NC].rearrange("p (t n) -> p t n", t=TT),
                  raw[:, D + TT * NC + NC:D + 2 * TT * NC + NC].rearrange("p (t n) -> p t n", t=TT),
                  blk[1], stage]
        x_old = blk[0]
        gate_b = work[:, 2 * TT * NC:(2 * TT + 2) * NC].rearrange("p (k n) -> p k n", k=2)
        gate_bias = rope_a[:, :]
        ws_t = sb("ws_t", [P, 1024])
        sp_bufs = [stage[:, 0:4, :].rearrange("p t n -> p (t n)"), work[:, 0:D]]
        h5 = work[:, 5120:5120 + NTOK]
        junk = wT[0][:, 0:2, :].rearrange("p k q -> p (k q)")
        ssq = sb("ssq", [P, 20])
        rstd = sb("rstd", [P, TT])
        wts_p = sb("wts_p", [P, P])
        sums = ssq[:, 0:10]
        inv_sums = ssq[:, 10:20]
        squares = [at.rearrange("p (t d) -> p t d", t=TT) for at in (weights[:, 0, :], ws_t[:, 0:640])]

        ps = ctx.enter_context(nc.psum_tensor("ps", [P, 8, NC], F32))
        TURN = 5
        SC = 6
        MOD = 6
        MOD_ROWS = (7, 5)
        turned = ps[:, TURN:TURN + 2, :].rearrange("p a b -> p (a b)")[:, 0:NTOK]

        def dram(name, shape):
            return nc.dram_tensor(name, shape, F32, kind="Internal").ap()

        z_d = [dram("z0", (11, P, TT, NC)), dram("z1", (16, P, TT, NC))]
        o_d = [dram("o0", (TT, P, D)), dram("o1", (TT, P, D))]
        kn_d = dram("kn", (L0.heads, P, P))
        x_d = dram("x1", (TT, P, D))
        x2_d = dram("x2", (TT, P, D))

        w_landed = [sem(f"w_landed{i}") for i in range(RAW)]
        raw_taken = sem("raw_taken")
        pool_passed = sem("pool_passed")
        w_hi_ready = sem("w_hi_ready")
        w_lo_ready = sem("w_lo_ready")
        w_used = sem("w_used")
        acc_ready = sem("acc_ready")
        acc_free = sem("acc_free")
        mod_free = sem("mod_free")
        stage_full = sem("stage_full")
        stage_stored = sem("stage_stored")
        stage_free = sem("stage_free")
        row_ready = sem("row_ready")
        mod_ready = sem("mod_ready")
        setup_in = sem("setup_in")
        setup_pe = sem("setup_pe")
        setup_act = sem("setup_act")
        setup_dve = sem("setup_dve")
        xt_in = sem("xt_in")
        sq_done = sem("sq_done")
        out_done = sem("out_done")
        x_in = [sem(f"x_in{n}") for n in range(2)]
        o_in = [sem(f"o_in{n}") for n in range(2)]
        g_in = sem("g_in")
        tanh_done = sem("tanh_done")
        src_ready = sem("src_ready")
        turn_ready = sem("turn_ready")
        turn_mid = sem("turn_mid")
        turn_hi = sem("turn_hi")
        turn_free = sem("turn_free")
        sp_in = sem("sp_in")
        sp_last_in = sem("sp_last_in")
        vn_ready = sem("vn_ready")
        sp_ready = sem("sp_ready")
        sp_free = sem("sp_free")
        sp_stored = sem("sp_stored")
        gb_in = sem("gb_in")
        gb_free = sem("gb_free")
        xo_in = sem("xo_in")
        xo_free = sem("xo_free")
        kn_stored = sem("kn_stored")
        fg_in = sem("fg_in")
        fin_in = [sem(f"fin_in{n}") for n in range(3)]
        fin_ready = sem("fin_ready")
        fin_stored = sem("fin_stored")
        copied = sem("copied")

        class AttnSems:
            def __init__(self, l):
                s = lambda n: sem(f"{n}_{l}")
                self.qk_in = s("qk_in")
                self.v_in = s("v_in")
                self.normed = s("head_normed")
                self.roped = s("head_roped")
                self.t_ready = s("t_ready")
                self.t_hi = s("t_hi")
                self.t_free = s("t_free")
                self.v_hi = s("v_hi")
                self.v_split = s("v_split")
                self.s_ready = s("s_ready")
                self.s_max = s("s_max")
                self.s_exp = s("s_exp")
                self.w_ready = s("w_ready")
                self.pv_ready = s("pv_ready")
                self.pv_copied = s("pv_copied")
                self.b_ready = s("b_ready")
                self.o_done = s("o_done")
                self.o_stored = s("o_stored")
                self.o_free = s("o_free")

        S = [AttnSems(0), AttnSems(1)]
        block = ctx.enter_context(nc.Block())

        w_units = {}

        def unit(name, i):
            if name not in w_units:
                w_units[name] = a[name].rearrange("(u k p) n -> u p k n", k=2, p=P)
            return w_units[name][i]

        @block.sync
        def _(sp):
            def load_chunk(c, name, col, first=False):
                for i in range(UNITS):
                    if not first:
                        sp.wait_ge(w_lo_ready, c * KT + (2 * i + 2 - KT))
                        sp.sem_inc(raw_taken, 1)
                    sp.dma_start(w_raw[:, i % RAW, :, :], unit(name, i)[:, :, bass.ds(col, NC)]).then_inc(
                        w_landed[i % RAW], 16)

            rows = [("c", 0, 16, "o (r d) -> (o r) d"), ("c_ctx", 16, 16, "(r d) -> r d"),
                    ("norm_g0", 32, 16, "(r d) -> r d"), ("norm_g1", 48, 16, "(r d) -> r d")]
            for name, at, n, how in rows:
                sp.dma_start(area[at:at + n, 0, 0:P], a[name].rearrange(how, d=P)).then_inc(setup_in, 16)
            for l in range(2):
                sp.dma_start(area[64 + 32 * l:96 + 32 * l, 0, 0:P],
                             a[f"b_ada{l}"][0:2 * D].rearrange("(r d) -> r d", d=P)).then_inc(setup_in, 16)
            sp.dma_start(consts[:, :], a["layout"][:, 0:386]).then_inc(setup_in, 16)
            sp.dma_start(rope_c[:, :], a["rope"][0, 0]).then_inc(setup_in, 16)
            sp.dma_start(rope_s[:, :], a["rope"][0, 1]).then_inc(setup_in, 16)
            for t, name in ((gq, "q_norm_g0"), (gk, "k_norm_g0"), (gsub, "subln_g1")):
                sp.dma_start(t[:, :], a[name].unsqueeze(0).to_broadcast([P, P])).then_inc(setup_in, 16)
            for n, name in enumerate(("lambda_q1", "lambda_k1", "lambda_q2", "lambda_k2")):
                sp.dma_start(lam4[:, n, :], a[name].unsqueeze(0).to_broadcast([P, 64])).then_inc(setup_in, 16)
            sp.dma_start(area[0:8, 0, P:2 * P], a["b_s0"]).then_inc(setup_in, 16)
            sp.dma_start(area[:, 1, 0:1024].rearrange("p (g q) -> p g q", g=8),
                         a["w_s0"].rearrange("g p q -> p g q")).then_inc(setup_in, 16)

            load_chunk(0, "w_ada0", 0, first=True)
            with sp.Fori(1, 8) as i:
                load_chunk(i, "w_ada0", i * NC)
            load_chunk(C_L0, "w_in0", 4096)
            with sp.Fori(0, 2) as i:
                load_chunk(i + (C_L0 + 1), "w_in0", i * NC + 3072)
            with sp.Fori(0, 8) as i:
                load_chunk(i * 2 + C_L0I, "w_ada1", i * NC)
                load_chunk(i * 2 + (C_L0I + 1), "w_in0", i * NC + (i // 6) * 1536)
            with sp.Fori(0, 4) as j:
                load_chunk(j * 2 + C_O0, "w_ada0", j * NC + 2 * D)
                load_chunk(j * 2 + (C_O0 + 1), "w_out0", j * NC)
            with sp.Fori(0, 4) as g:
                for n in range(3):
                    load_chunk(g * 3 + (C_L1 + n), "w_in1", g * NC + n * D)
            with sp.Fori(0, 4) as i:
                load_chunk(i + (C_L1 + 12), "w_in1", i * NC + 3 * D)
            with sp.Fori(0, 4) as j:
                load_chunk(j * 2 + C_O1, "w_ada1", j * NC + 2 * D)
                load_chunk(j * 2 + (C_O1 + 1), "w_out1", j * NC)

        class Pace:

            def __init__(self, at, per):
                self.at, self.per = at, per

            def due(self, slot):
                return sum(1 for x in self.at if x == slot % self.per)

            def due_in(self, n, kt):
                return sum(self.due(n * SLOTS + kt * TT + t) for t in range(TT))

        pace0 = Pace(AT0, SLOTS)
        pace0s = Pace(AT0S, SLOTS)
        pace0t = Pace(AT0T, SLOTS)
        pace1 = Pace(AT1, 60)
        pace1g = Pace([x * 6 // 5 for x in AT1], SLOTS)

        def slot(F, b):
            return blk[(b + (F == 2)) % 2]

        def wait_slot_used(eng, c, kt):
            k = kt - RING
            if k >= 0:
                eng.wait_ge(w_used, c * 15 + (k + 1 + W_CREDIT))
            elif k == -1:
                eng.wait_ge(acc_ready, c * 5 + ACC_CREDIT)
            else:
                eng.wait_ge(w_used, (c - 1) * 15 + (KT + k + 1 + W_CREDIT))

        def attention_pe(pe, L, h, order=None, tiles=()):
            s = S[L.n]
            NT, NS, NF = L.n_turn, L.n_scores, L.n_bank

            spatial = [0]

            def bank_free(q):
                pe.wait_ge(s.t_free, h * NF + (q + 1))
                if spatial[0] > 0:
                    pe.wait_ge(sp_free, tiles[0] * 2 + spatial[0])

            def turn(q, blocks):
                bank_free(q)
                for n, src in enumerate(blocks):
                    last = nc.tensor.transpose(ps[:, TURN, n * P:(n + 1) * P], src, ident)
                last.then_inc(s.t_ready, 1)

            def scores(n, q0, halves):
                r0 = (n % L.maps) * L.dk
                pe.wait_ge(s.s_exp, h * NS + (n + 1))
                for b, (k0, w) in enumerate(halves):
                    for i, (x, y) in enumerate(((0, 0), (0, 1), (1, 0))):
                        last = nc.tensor.matmul(ps[:, SC + b, 0:w], qT[x][r0:r0 + L.dk, q0:q0 + P],
                                                kT[y][r0:r0 + L.dk, k0:k0 + w], start=(i == 0), stop=(i == 2))
                last.then_inc(s.s_ready, 1)

            def products(q, width, tiles):
                bank_free(q)
                for k, vt in enumerate(tiles):
                    for i, (x, y) in enumerate(((0, 0), (0, 1), (1, 0))):
                        last = nc.tensor.matmul(ps[:, TURN, 0:width], vv[x][:, vt, :], wT[y][:, k, 0:width],
                                                start=(k == 0 and i == 0), stop=(k == len(tiles) - 1 and i == 2))
                last.then_inc(s.pv_ready, 1)

            def back(n, count):
                pe.wait_ge(s.pv_copied, h * 3 + (n + 1))
                for i in range(count):
                    last = nc.tensor.transpose(ps[:, TURN, i * P:(i + 1) * P], oT[:, i * P:(i + 1) * P], ident)
                last.then_inc(s.b_ready, 1)

            r = n = p = b = q = 0
            for kind in order or L.order:
                if kind == "T":
                    if r == 0:
                        pe.wait_ge(s.roped, h + 1)
                        blocks = [q_in[:, t, :] for t in range(TS)]
                    elif r == 1:
                        blocks = [k_in[:, t, :] for t in range(TS)]
                    elif r == 2:
                        blocks = [q_in[:, TS, :], ck_in, k_in[:, TS, :]]
                    elif r < 9:
                        tile = 2 * (r // 3 - 1)
                        if r % 3 == 0:
                            if L.maps == 1:
                                pe.wait_ge(s.s_exp, h * NS + (tile + 3))
                            else:
                                pe.wait_ge(s.w_ready, h * 5 + (tile + 3))
                        at = tile if L.maps == 1 else 2
                        blocks = [weights[:, at + i, k * P:(k + 1) * P] for k in ((0, 1), (2, 3), (4,))[r % 3]
                                  for i in range(2)]
                    else:
                        if L.maps == 1:
                            pe.wait_ge(s.s_exp, h * NS + 6)
                        else:
                            pe.wait_ge(s.w_ready, h * 5 + 6)
                        blocks = [wts_p[:, :]]
                    turn(q, blocks)
                    r, q = r + 1, q + 1
                elif kind == "S":
                    if n == 0:
                        pe.wait_ge(s.t_free, h * NF + 4)
                        if L.n == 0:
                            pe.wait_ge(mod_free, h + 10)
                    if n < TS * L.maps:
                        scores(n, n // L.maps * P, ((0, 320), (320, 320)))
                    else:
                        scores(n, TS * P, ((NTOK, P),))
                    n += 1
                elif kind == "P":
                    if p == 0:
                        pe.wait_ge(s.v_split, h + 1)
                    if p < 2:
                        products(q, 256, [0, 1, 2, 3, 5])
                    else:
                        products(q, P, [4])
                    p += 1
                elif kind == "B":
                    back(b, 2 if b < 2 else 1)
                    b, q = b + 1, q + 1
                elif kind == "G":
                    x, half = spatial[0] // 2, spatial[0] % 2
                    pe.wait_ge(vn_ready, tiles[x] + 1)
                    bank_free(q)
                    for g in range(4):
                        at = (half * 4 + g) * P
                        last = nc.tensor.matmul(ps[:, TURN, g * P:(g + 1) * P], ws_t[:, at:at + P],
                                                sp_bufs[x][:, at:at + P], start=True, stop=True)
                    last.then_inc(sp_ready, 1)
                    spatial[0] += 1
                yield

        @block.tensor
        def _(pe):
            def feed_turn(F, kt):
                if kt % 4 == 0:
                    pe.wait_ge(src_ready, 4 * F + kt // 4 + 1)
                if kt > 0 and F % 2 == 0:
                    pe.wait_ge(turn_mid, 8 * F + kt)
                elif kt > 0:
                    pe.wait_ge(turn_free, 16 * F + kt)
                for t in range(TT):
                    last = nc.tensor.transpose(ps[:, TURN + t // TS, t % TS * P:(t % TS + 1) * P],
                                               slot(F, kt // 4)[:, t, kt % 4 * P:(kt % 4 + 1) * P], ident)
                last.then_inc(turn_ready, 1)

            def project_chunk(c, n, step=None, F=None):
                if F is not None:
                    for kt in range(FEED):
                        feed_turn(F, kt)
                for kt in range(KT):
                    if F is not None:
                        if kt + FEED < KT:
                            feed_turn(F, kt + FEED)
                        pe.wait_ge(turn_free, 16 * F + kt + 1)
                    pe.wait_ge(w_lo_ready, c * KT + (kt + 1))
                    for t in range(TT):
                        if kt == 0:
                            pe.wait_ge(acc_free, n * 5 + (t + 1))
                        for i, (x, w) in enumerate(((hT_hi, w_hi), (hT_hi, w_lo), (hT_lo, w_hi))):
                            last = nc.tensor.matmul(ps[:, t, :], x[:, kt, t * P:(t + 1) * P], w[:, kt % RING, :],
                                                    start=(kt == 0 and i == 0), stop=(kt == KT - 1 and i == 2))
                        if kt == KT - 1:
                            last.then_inc(acc_ready, 1)
                        elif t == TT - 1:
                            last.then_inc(w_used, 1)
                        if step is not None:
                            step(kt * TT + t)

            def ada_products(c, n, before=None):
                if not isinstance(n, int) or n > 0:
                    pe.wait_ge(row_ready, n)
                for kt in range(KT):
                    if kt == 2 and before is not None:
                        ada_finish(before, False)
                    pe.wait_ge(w_lo_ready, c * KT + (kt + 1))
                    for i, w in enumerate((w_hi, w_lo)):
                        last = nc.tensor.matmul(ps[:, MOD, :], cst[:, kt * 4:kt * 4 + P], w[:, kt % RING, :],
                                                start=(kt == 0 and i == 0), stop=(kt == KT - 1 and i == 1))
                    last.then_inc(*((acc_ready, 5) if kt == KT - 1 else (w_used, 1)))

            def ada_finish(n, gate):
                pe.wait_ge(row_ready, n + 1)
                pe.wait_ge(mod_free, n + 1)
                if gate:
                    for k in range(2):
                        last = nc.tensor.matmul(ps[:, MOD_ROWS[k], :], sel_row[k], modrow[:, :], start=True, stop=True)
                else:
                    for k in range(4):
                        last = nc.tensor.matmul(ps[:, MOD_ROWS[0], 2 * k:2 * k + 2], modrow[:, k * P:(k + 1) * P],
                                                sel_col, start=True, stop=True)
                last.then_inc(mod_ready, 1)

            def finish_early(n, gate, step=None):
                def both(slot):
                    if slot == 2:
                        ada_finish(n, gate)
                    if step is not None:
                        step(slot)
                return both

            def stepper(steps, pace, n=0):
                def step(slot):
                    for _ in range(pace.due(n * SLOTS + slot)):
                        next(steps, None)
                return step

            def finish(steps):
                for _ in steps:
                    pass

            pe.sem_inc(w_used, W_CREDIT)
            pe.sem_inc(acc_ready, ACC_CREDIT)
            pe.wait_ge(setup_in, 16 * N_SETUP)
            nc.tensor.transpose(ps[:, 7, 0:P], area[:, 0, 0:P], ident)
            nc.tensor.transpose(ps[:, 7, P:P + 8], area[0:8, 0, P:2 * P], ident[0:8, 0:8])
            for g in range(8):
                last = nc.tensor.transpose(ps[:, 5 + g // 4, (g % 4) * P:(g % 4 + 1) * P],
                                           area[:, 1, g * P:(g + 1) * P], ident)
            last.then_inc(setup_pe, 1)
            pe.wait_ge(setup_dve, 1)
            ada_products(0, 0)
            with pe.Fori(1, 8) as i:
                ada_products(i, i, before=i - 1)
            ada_finish(7, False)
            project_chunk(C_L0, 0, F=0)
            with pe.Fori(0, 2) as i:
                project_chunk(i + (C_L0 + 1), i + 1)

            def pair0(i, pace, order=None, tiles=()):
                ada_products(i * 2 + C_L0I, i + 8)
                steps = attention_pe(pe, L0, i, order, tiles)
                project_chunk(i * 2 + (C_L0I + 1), i + 3, finish_early(i + 8, False, stepper(steps, pace)))
                finish(steps)

            with pe.Fori(0, 4) as i:
                pair0(i, pace0)
            with pe.Fori(4, 7) as i:
                pair0(i, pace0s, ORDER0S, [i - 4])
            pair0(7, pace0t, ORDER0T, [3, 4])
            ada_products(C_O0, 16)
            pe.wait_ge(sp_free, 10)
            pe.wait_ge(S[0].t_free, 8 * L0.n_bank + 1)
            ada_finish(16, True)
            pe.wait_ge(mod_free, 18)
            project_chunk(C_O0 + 1, 11, F=1)
            with pe.Fori(1, 4) as j:
                ada_products(j * 2 + C_O0, j + 16)
                project_chunk(j * 2 + (C_O0 + 1), j + 11, finish_early(j + 16, True))
            project_chunk(C_L1, 15, F=2)
            with pe.Fori(1, 3) as i:
                project_chunk(i + C_L1, i + 15)
            with pe.Fori(0, 3) as g:
                steps = chain(attention_pe(pe, L1, g * 4 + x) for x in range(4))
                for n in range(3):
                    project_chunk(g * 3 + (C_L1 + 3 + n), g * 3 + (18 + n), stepper(steps, pace1, n))
                finish(steps)
            with pe.Fori(0, 4) as j:
                steps = attention_pe(pe, L1, j + 12)
                project_chunk(j + (C_L1 + 12), j + 27, stepper(steps, pace1g))
                finish(steps)
            ada_products(C_O1, 20)
            pe.wait_ge(S[1].t_free, 16 * L1.n_bank + 1)
            ada_finish(20, True)
            pe.wait_ge(mod_free, 22)
            project_chunk(C_O1 + 1, 31, F=3)
            with pe.Fori(1, 4) as j:
                ada_products(j * 2 + C_O1, j + 20)
                project_chunk(j * 2 + (C_O1 + 1), j + 31, finish_early(j + 20, True))

        def attention_act(act, L, h, order=None):
            s = S[L.n]
            NT, NS = L.n_turn, L.n_scores

            def turn(r, pieces):
                act.wait_ge(s.t_ready, h * NT + (r + 1))
                for (c0, c1), dst in pieces:
                    last = nc.scalar.copy(dst, ps[:, TURN, c0:c1])
                last.then_inc(s.t_hi, 1)

            def scores(n, u, src, width):
                m = n % L.maps
                if m == 0 and L.maps == 2:
                    act.wait_ge(s.w_ready, h * 5 + (u + 1))
                act.wait_ge(s.s_max, h * NS + (n + 1))
                dst = weights[:, m if L.maps == 2 else u, :] if L.maps == 2 or u < TS else wts_p
                dst = dst[:, 0:width]
                nc.scalar.activation(dst if src.ndim == 2 else dst.rearrange("p (b w) -> p b w", b=2),
                                     src, ACT.Exp, bias=small[:, 20 + m:21 + m], scale=L.scale,
                                     accum_out=sums[:, n:n + 1]).then_inc(s.s_exp, 1)

            flat = "p k q -> p (k q)"
            w_pieces = [[((0, 512), wT[0][:, 0:2, :].rearrange(flat))], [((0, 512), wT[0][:, 2:4, :].rearrange(flat))],
                        [((0, 256), wT[0][:, 4, :])]]
            pieces = ([[((0, 512), qT[0][:, 0:512])], [((0, 512), kT[0][:, 0:512])],
                       [((0, 128), qT[0][:, 512:640]), ((128, 384), kT[0][:, 512:768])]]
                      + w_pieces + w_pieces + [[((0, P), wT[0][:, 0, 0:P])]])
            r = n = p = 0
            for kind in order or L.order:
                if kind == "T":
                    if r == 3:
                        act.wait_ge(s.v_in, h * 32 + 32)
                        nc.scalar.copy(vv[0][:, 0:TT, :], v_in[:, :, :])
                        nc.scalar.copy(vv[0][:, TT, :], cv_in[:, :]).then_inc(s.v_hi, 1)
                    turn(r, pieces[r])
                    r += 1
                elif kind == "S":
                    if n < TS * L.maps:
                        scores(n, n // L.maps, ps[:, SC:SC + 2, 0:320], 640)
                    else:
                        scores(n, TS, ps[:, SC, 0:P], P)
                    n += 1
                elif kind == "P":
                    width = 256 if p < 2 else P
                    act.wait_ge(s.pv_ready, h * 3 + (p + 1))
                    nc.scalar.copy(oT[:, 0:width], ps[:, TURN, 0:width]).then_inc(s.pv_copied, 1)
                    p += 1
                yield

        @block.scalar
        def _(act):
            def split_hi(c, kt):
                i = kt // 2
                act.wait_ge(w_landed[i % RAW], c * 16 * (UNITS // RAW) + 16 * (i // RAW + 1))
                wait_slot_used(act, c, kt)
                nc.scalar.copy(w_hi[:, kt % RING, :], w_raw[:, i % RAW, kt % 2, :]).then_inc(w_hi_ready, 1)

            def split_chunk(c, beside=None, last=False):
                for kt in range(KT):
                    k = kt + AHEAD
                    if k < KT:
                        split_hi(c, k)
                    elif not last:
                        split_hi(c + 1, k - KT)
                    if beside is not None:
                        beside(kt)

            def evacuate(c, n, step=None):
                act.wait_ge(stage_free, n + 1)
                for t in range(TT):
                    act.wait_ge(acc_ready, c * 5 + (t + 1 + ACC_CREDIT))
                    nc.scalar.copy(stage[:, t, :], ps[:, t, :]).then_inc(acc_free, 1)
                    if step is not None:
                        step(t)
                act.drain().then_inc(stage_full, 1)

            def evacuate_gate(c, n):
                act.wait_ge(stage_free, n + 1)
                for t in range(TT):
                    act.wait_ge(acc_ready, c * 5 + (t + 1 + ACC_CREDIT))
                    nc.scalar.activation(stage[:, t, :], ps[:, t, :], ACT.Tanh, scale=0.5).then_inc(tanh_done, 1)

            def feed_hi(F, kt):
                if F % 2 == 0:
                    act.wait_ge(turn_mid, 8 * F + kt + 1)
                    src = h5
                else:
                    act.wait_ge(turn_ready, 16 * F + kt + 1)
                    src = turned
                nc.scalar.copy(hT_hi[:, kt, :], src).then_inc(turn_hi, 1)

            def feed_beside(F):
                return lambda kt: feed_hi(F, kt + FEED) if kt + FEED < KT else None

            def square_tile(n, m):
                act.drain()
                act.wait_ge(out_done, n * TT + m + 1)
                nc.scalar.activation(junk, stage[:, m, :], ACT.Square,
                                     accum_out=ssq[:, bass.ds((n % 4) * TT + m, 1)]).then_inc(sq_done, 1)

            def stepper(steps, pace, n=0):
                def beside(kt):
                    for _ in range(pace.due_in(n, kt)):
                        next(steps, None)
                return beside

            def finish(steps):
                for _ in steps:
                    pass

            act.wait_ge(setup_pe, 1)
            nc.scalar.copy(vcol[:, :], ps[:, 7, 0:P])
            nc.scalar.copy(bsT[:, :], ps[:, 7, P:P + 8])
            nc.scalar.copy(ws_t[:, :], ps[:, 5:7, :].rearrange("p a b -> p (a b)"))
            act.drain().then_inc(setup_act, 1)
            nc.scalar.activation(small[:, 64:96], vcol[:, 0:32], ACT.Tanh, scale=0.5).then_inc(setup_act, 1)
            act.wait_ge(setup_dve, 2)
            nc.scalar.activation(small[:, 10:12], small[:, 8:10], ACT.Exp).then_inc(setup_act, 1)
            act.sem_inc(S[0].s_exp, 1)
            act.sem_inc(S[1].s_exp, 1)
            for kt in range(AHEAD):
                split_hi(0, kt)

            def square_x(t):
                act.drain()
                act.wait_ge(xt_in, t * 16 + 16)
                nc.scalar.activation(sp_bufs[0], area[:, 2, :], ACT.Square,
                                     accum_out=ssq[:, bass.ds(t, 1)]).then_inc(sq_done, 1)

            with act.Fori(0, 5) as i:
                split_chunk(i)
                square_x(i)
            with act.Fori(5, 8) as i:
                split_chunk(i)
            for kt in range(FEED):
                feed_hi(0, kt)
            split_chunk(C_L0, feed_beside(0))
            evacuate(C_L0, 0)
            with act.Fori(0, 2) as i:
                split_chunk(i + (C_L0 + 1))
                evacuate(i + (C_L0 + 1), i + 1)

            def pair0(i, pace, evac, order=None):
                split_chunk(i * 2 + C_L0I)
                steps = attention_act(act, L0, i, order)
                split_chunk(i * 2 + (C_L0I + 1), stepper(steps, pace))
                finish(steps)
                evac(i * 2 + (C_L0I + 1), i + 3)

            with act.Fori(0, 4) as i:
                pair0(i, pace0, evacuate)
            with act.Fori(4, 7) as i:
                pair0(i, pace0s, evacuate_gate, ORDER0S)
            pair0(7, pace0t, evacuate_gate, ORDER0T)

            def output(first, F, n0, last):
                split_chunk(first)
                for kt in range(FEED):
                    feed_hi(F, kt)
                split_chunk(first + 1, feed_beside(F))

                def output_pair(j, last=False):
                    split_chunk(j * 2 + first)
                    split_chunk(j * 2 + (first + 1),
                                lambda kt: square_tile(j + (n0 - 1), kt - 7) if 7 <= kt < 12 else None, last)
                with act.Fori(1, 3) as j:
                    output_pair(j)
                output_pair(3, last)
                for t in range(TT):
                    square_tile(n0 + 3, t)

            output(C_O0, 1, 0, False)
            for kt in range(FEED):
                feed_hi(2, kt)
            split_chunk(C_L1, feed_beside(2))
            evacuate(C_L1, 15)
            with act.Fori(1, 3) as i:
                split_chunk(i + C_L1)
                evacuate(i + C_L1, i + 15)
            with act.Fori(0, 3) as g:
                steps = chain(attention_act(act, L1, g * 4 + x) for x in range(4))
                for n in range(3):
                    def step(t, n=n):
                        for _ in range(pace1.due(n * SLOTS + SLOTS - TT + t)):
                            next(steps, None)

                    rows = stepper(steps, pace1, n)
                    split_chunk(g * 3 + (C_L1 + 3 + n), lambda kt: rows(kt) if kt < KT - 1 else None)
                    evacuate(g * 3 + (C_L1 + 3 + n), g * 3 + (18 + n), step)
                finish(steps)
            with act.Fori(0, 4) as j:
                steps = attention_act(act, L1, j + 12)
                split_chunk(j + (C_L1 + 12), stepper(steps, pace1g))
                finish(steps)
                evacuate_gate(j + (C_L1 + 12), j + 27)
            output(C_O1, 3, 4, True)

        def rsqrt_parts(dve, x, r, t):
            nc.vector.tensor_scalar(r.bitcast(I32), x.bitcast(I32), 1, None, ALU.logical_shift_right)
            dve.drain()
            nc.vector.tensor_scalar(r.bitcast(I32), r.bitcast(I32), -1.0, float(0x5F3759DF), ALU.mult, ALU.add)
            for _ in range(3):
                yield
                dve.drain()
                nc.vector.tensor_tensor(t, r, r, ALU.mult)
                dve.drain()
                nc.vector.scalar_tensor_tensor(t, t, -0.5, x, ALU.mult, ALU.mult)
                dve.drain()
                nc.vector.scalar_tensor_tensor(r, t, 1.5, r, ALU.add, ALU.mult)

        def rsqrt(dve, x, r, t):
            for _ in rsqrt_parts(dve, x, r, t):
                pass
            dve.drain()

        def norm_head(dve, h):
            s = S[0]
            dve.drain()
            dve.wait_ge(s.qk_in, h * 48 + 48)
            for n, z in enumerate((q_in, k_in)):
                if n == 1:
                    dve.drain()
                nc.vector.tensor_tensor(squares[0], z[:, :, :], z[:, :, :], ALU.mult)
                dve.drain()
                nc.vector.tensor_reduce(small[:, 40 + 5 * n:45 + 5 * n], squares[0], AX_X, ALU.add)
                yield
            dve.drain()
            nc.vector.tensor_scalar(small[:, 40:50], small[:, 40:50], 1.0 / P, EPS, ALU.mult, ALU.add)
            dve.drain()
            rsqrt(dve, small[:, 40:50], small[:, 50:60], small[:, 30:40])
            yield
            for n, (z, g) in enumerate(((q_in, gq), (k_in, gk))):
                nc.vector.tensor_tensor(z[:, :, :], z[:, :, :],
                                        small[:, 50 + 5 * n:55 + 5 * n].unsqueeze(2).to_broadcast([P, TT, P]), ALU.mult)
                dve.drain()
                last = nc.vector.tensor_tensor(z[:, :, :], z[:, :, :], g[:, :].unsqueeze(1).to_broadcast([P, TT, P]),
                                               ALU.mult)
                if n == 0:
                    yield
            dve.drain().then_inc(s.normed, 1)

        def norm_out(dve):
            x, r, t = small[:, 40:45], small[:, 50:55], small[:, 30:35]
            dve.drain()
            nc.vector.tensor_tensor(squares[1], o_head[:, :, :], o_head[:, :, :], ALU.mult)
            yield
            dve.drain()
            nc.vector.tensor_reduce(x, squares[1], AX_X, ALU.add)
            yield
            dve.drain()
            nc.vector.tensor_scalar(x, x, 1.0 / P, EPS, ALU.mult, ALU.add)
            dve.drain()
            yield from rsqrt_parts(dve, x, r, t)
            dve.drain()
            nc.vector.tensor_tensor(o_head[:, :, :], o_head[:, :, :], r.unsqueeze(2).to_broadcast([P, TT, P]), ALU.mult)
            yield
            dve.drain()
            nc.vector.tensor_tensor(o_head[:, :, :], o_head[:, :, :],
                                    gsub[:, :].unsqueeze(1).to_broadcast([P, TT, P]), ALU.mult)
            dve.drain().then_inc(S[1].o_done, 1)

        def heads_dve(dve, first, count):
            for x in range(count):
                yield from attention_dve(dve, L1, first + x, before=norm_out(dve))

        def attention_dve(dve, L, h, order=None, tiles=(), last_head=False, before=None):
            s = S[L.n]
            NT, NS = L.n_turn, L.n_scores

            def turn(r, pieces):
                dve.wait_ge(s.t_hi, h * NT + (r + 1))
                for (c0, c1), hi, lo in pieces:
                    last_op = nc.vector.tensor_tensor(lo, ps[:, TURN, c0:c1], hi.bitcast(F32), ALU.subtract)
                last_op.then_inc(s.t_free, 1)

            def scores(n, src):
                m = n % L.maps
                dve.drain()
                dve.wait_ge(s.s_ready, h * NS + (n + 1))
                nc.vector.tensor_reduce(small[:, 22 + m:23 + m], src,
                                        AX_X if src.ndim == 2 else mybir.AxisListType.XY, ALU.max)
                dve.drain()
                nc.vector.tensor_scalar(small[:, 20 + m:21 + m], small[:, 22 + m:23 + m], -L.scale, None,
                                        ALU.mult).then_inc(s.s_max, 1)

            def combine(u):
                width = 640 if u < TS else P
                dst = weights[:, 2 + u % 2, :] if u < TS else wts_p[:, :]
                dve.drain()
                dve.wait_ge(s.s_exp, h * NS + ((u + 1) * L.maps + 1))
                nc.vector.reciprocal(inv_sums[:, 2 * u:2 * u + 2], sums[:, 2 * u:2 * u + 2])
                dve.drain()
                nc.vector.scalar_tensor_tensor(small[:, 26:27], sums[:, 2 * u:2 * u + 1], small[:, 12:13],
                                               inv_sums[:, 2 * u + 1:2 * u + 2], ALU.mult, ALU.mult)
                dve.drain()
                nc.vector.scalar_tensor_tensor(dst, weights[:, 1, 0:width], small[:, 26:27], weights[:, 0, 0:width],
                                               ALU.mult, ALU.add).then_inc(s.w_ready, 1)

            def back(n, t0, count):
                dve.drain()
                if L.maps == 1:
                    dve.wait_ge(s.s_exp, h * NS + (t0 + count + 1))
                    nc.vector.reciprocal(inv_sums[:, t0:t0 + count], sums[:, t0:t0 + count])
                    dve.drain()
                dve.wait_ge(s.b_ready, h * 3 + (n + 1))
                if n == 0:
                    dve.wait_ge(s.o_free, h + 1)
                for k in range(count):
                    at = (t0 + k) * L.maps
                    last_op = nc.vector.tensor_scalar(o_head[:, t0 + k, :], ps[:, TURN, k * P:(k + 1) * P],
                                                      inv_sums[:, at:at + 1], None, ALU.mult)
                last_op.then_inc(s.t_free, 1)

            flat = "p k q -> p (k q)"
            w_pieces = [[((0, 512),) + tuple(w[:, 0:2, :].rearrange(flat) for w in wT)],
                        [((0, 512),) + tuple(w[:, 2:4, :].rearrange(flat) for w in wT)],
                        [((0, 256), wT[0][:, 4, :], wT[1][:, 4, :])]]
            pieces = ([[((0, 512), qT[0][:, 0:512], qT[1][:, 0:512])], [((0, 512), kT[0][:, 0:512], kT[1][:, 0:512])],
                       [((0, 128), qT[0][:, 512:640], qT[1][:, 512:640]),
                        ((128, 384), kT[0][:, 512:768], kT[1][:, 512:768])]]
                      + w_pieces + w_pieces + [[((0, P), wT[0][:, 0, 0:P], wT[1][:, 0, 0:P])]])
            next_norm = norm_head(dve, h + 1) if L.n == 0 and not last_head else iter(())
            r = n = p = b = u = 0
            normed = spatial = 0
            for kind in order or L.order:
                if kind == "T":
                    if r == 3:
                        if L.maps == 2:
                            combine(1)
                            u = 2
                        dve.wait_ge(s.v_hi, h + 1)
                        nc.vector.tensor_tensor(vv[1][:, 0:TT, :], v_in[:, :, :], vv[0][:, 0:TT, :].bitcast(F32),
                                                ALU.subtract)
                        nc.vector.tensor_tensor(vv[1][:, TT, :], cv_in[:, :], vv[0][:, TT, :].bitcast(F32),
                                                ALU.subtract)
                        dve.drain().then_inc(s.v_split, 1)
                    turn(r, pieces[r])
                    r += 1
                elif kind == "S":
                    if L.maps == 2 and n % L.maps == 0 and n // L.maps > u:
                        combine(u)
                        u += 1
                    scores(n, ps[:, SC:SC + 2, 0:320] if n < TS * L.maps else ps[:, SC, 0:P])
                    n += 1
                elif kind == "P":
                    p += 1
                    if L.maps == 2 and p == 2:
                        combine(4)
                elif kind == "B":
                    back(b, 2 * b, 2 if b < 2 else 1)
                    b += 1
                elif kind == "L":
                    va = sp_bufs[normed][:, 0:1024]
                    dve.drain()
                    if normed == 0:
                        dve.wait_ge(sp_in, tiles[0] * 32 + 32)
                    else:
                        dve.wait_ge(sp_last_in, 32)
                    for k in range(2):
                        nc.vector.bn_stats(small[:, 60 + 6 * k:66 + 6 * k], va[:, k * NC:(k + 1) * NC])
                    dve.drain()
                    nc.vector.bn_aggr(small[:, 72:74], small[:, 60:72])
                    dve.drain()
                    nc.vector.tensor_scalar(small[:, 74:75], small[:, 73:74], EPS, None, ALU.add)
                    dve.drain()
                    rsqrt(dve, small[:, 74:75], small[:, 75:76], small[:, 76:77])
                    nc.vector.tensor_scalar(va, va, small[:, 72:73], small[:, 75:76], ALU.subtract,
                                            ALU.mult).then_inc(vn_ready, 1)
                    normed += 1
                elif kind == "G":
                    buf, half = sp_bufs[spatial // 2], spatial % 2
                    dve.wait_ge(sp_ready, tiles[0] * 2 + (spatial + 1))
                    for g in range(half * 4, half * 4 + 4):
                        y = buf[:, 1024 + g * P:1024 + (g + 1) * P]
                        nc.vector.scalar_tensor_tensor(y, ps[:, TURN, g % 4 * P:(g % 4 + 1) * P], bsT[:, g:g + 1], y,
                                                       ALU.add, ALU.mult)
                    dve.drain().then_inc(sp_free, 1)
                    spatial += 1
                if r >= 8:
                    next(next_norm, None)
                if before is not None and not 3 <= n <= 4:
                    next(before, None)
                if b == 3 and L.n == 0:
                    for _ in next_norm:
                        pass
                    dve.drain().then_inc(s.o_done, 1)
                yield

        @block.vector
        def _(dve):
            def split_lo(c, kt):
                i = kt // 2
                dve.wait_ge(w_hi_ready, c * KT + (kt + 1))
                nc.vector.tensor_tensor(w_lo[:, kt % RING, :], w_raw[:, i % RAW, kt % 2, :],
                                        w_hi[:, kt % RING, :].bitcast(F32), ALU.subtract).then_inc(w_lo_ready, 1)

            def split_chunk(c, beside=None, last=False):
                for kt in range(KT):
                    k = kt + AHEAD
                    if k < KT:
                        split_lo(c, k)
                    elif not last:
                        split_lo(c + 1, k - KT)
                    if beside is not None:
                        beside(kt)

            def evacuate_gate(c, n, m):
                for t in range(TT):
                    dve.wait_ge(tanh_done, m * TT + (t + 1))
                    nc.vector.scalar_tensor_tensor(stage[:, t, :], stage[:, t, :], 1.0, ps[:, t, :], ALU.add,
                                                   ALU.mult).then_inc(acc_free, 1)
                dve.drain().then_inc(stage_full, 1)

            def ada_rows(c):
                dve.wait_ge(acc_ready, c * 5 + (5 + ACC_CREDIT))
                nc.vector.tensor_copy(modrow[:, :], ps[0:4, MOD, :]).then_inc(row_ready, 1)

            def ada_columns(n, l, i):
                dve.wait_ge(mod_ready, n + 1)
                nc.vector.tensor_tensor(modcol[l][:, bass.ds(i * 4, 4), :],
                                        ps[:, MOD_ROWS[0], 0:8].rearrange("p (k c) -> p k c", c=2),
                                        vcol[:, bass.ds(i * 4 + (64 + 32 * l), 4)].unsqueeze(2).to_broadcast([P, 4, 2]),
                                        ALU.add).then_inc(mod_free, 1)

            def ada_gate(n, m):
                dve.drain()
                dve.wait_ge(mod_ready, n + 1)
                dve.wait_ge(gb_in, m * 16 + 16)
                for k in range(2):
                    nc.vector.tensor_tensor(gate_b[:, k, :], ps[:, MOD_ROWS[k], :], gate_bias, ALU.add)
                dve.drain().then_inc(gb_free, 1)
                dve.drain().then_inc(mod_free, 1)

            def scale_columns(l):
                dve.drain()
                nc.vector.scalar_tensor_tensor(modcol[l][:, 16:32, :], modcol[l][:, 16:32, :], 1.0,
                                               vcol[:, 32 + 16 * l:48 + 16 * l].unsqueeze(2).to_broadcast([P, 16, 2]),
                                               ALU.add, ALU.mult)
                dve.drain()

            def row_norms(partial):
                dve.drain()
                if partial:
                    nc.vector.tensor_reduce(small[:, 60:65], ssq[:, :].rearrange("p (j t) -> p t j", j=4), AX_X,
                                            ALU.add)
                    dve.drain()
                src = small[:, 60:65] if partial else ssq[:, 0:TT]
                nc.vector.tensor_scalar(small[:, 65:70], src, 1.0 / D, EPS, ALU.mult, ALU.add)
                dve.drain()
                rsqrt(dve, small[:, 65:70], rstd[:, :], small[:, 70:75])

            def feed_block(F, b):
                x = slot(F, b)
                if F % 2 == 0:
                    dve.wait_ge(x_in[b % 2], F * 32 + (b // 2 + 1) * 32)
                    for t in range(TT):
                        nc.vector.tensor_scalar(x[:, t, :], x[:, t, :], rstd[:, t:t + 1], None, ALU.mult)
                else:
                    dve.wait_ge(o_in[b % 2], F // 2 * 32 + (b // 2 + 1) * 16)
                    dve.wait_ge(g_in, F // 2 * 64 + (b + 1) * 16)
                    nc.vector.scalar_tensor_tensor(x, stage[:, :, :] if b > 0 else blk[1], 0.5, x, ALU.mult, ALU.mult)
                dve.drain().then_inc(src_ready, 1)

            def feed_lo(F, kt):
                src = h5 if F % 2 == 0 else turned
                dve.wait_ge(turn_hi, 16 * F + kt + 1)
                nc.vector.tensor_tensor(hT_lo[:, kt, :], src, hT_hi[:, kt, :].bitcast(F32),
                                        ALU.subtract).then_inc(turn_free, 1)

            def feed_step(F, k):
                if k == 0:
                    feed_block(F, 0)
                if F % 2 == 1 and k < KT:
                    feed_lo(F, k)
                if F % 2 == 0 and k > 0:
                    feed_lo(F, k - 1)
                if F % 2 == 0 and k < KT:
                    dve.drain()
                    dve.wait_ge(turn_ready, 16 * F + k + 1)
                    for cond, (c0, c1) in enumerate(((0, TS * P), (TS * P, NTOK))):
                        nc.vector.tensor_scalar(h5[:, c0:c1], turned[:, c0:c1],
                                                modcol[F // 2][:, 16 + k, cond:cond + 1],
                                                modcol[F // 2][:, k, cond:cond + 1], ALU.mult, ALU.add)
                    dve.drain().then_inc(turn_mid, 1)
                if k % 4 == 3 and k + 1 < KT:
                    feed_block(F, (k + 1) // 4)

            def feed_beside(F):
                return lambda kt: feed_step(F, kt + FEED) if kt + FEED <= KT else None

            def stepper(steps, pace, n=0, first=None):
                def beside(kt):
                    if kt == 0 and first is not None:
                        first()
                    for _ in range(pace.due_in(n, kt)):
                        next(steps, None)
                return beside

            def finish(steps):
                for _ in steps:
                    pass

            dve.sem_inc(acc_free, 5)
            dve.sem_inc(mod_free, 1)
            for s in S:
                dve.sem_inc(s.t_free, 1)
                dve.sem_inc(s.w_ready, 1)
            nc.vector.memset(cst[:, :].bitcast(F32), 0.0)
            dve.wait_ge(setup_act, 2)
            nc.vector.scalar_tensor_tensor(small[:, 32:64], small[:, 64:96], 1.0, vcol[:, 0:32], ALU.add, ALU.mult)
            dve.drain()
            nc.vector.tensor_scalar(small[:, 32:64], small[:, 32:64], 0.5, None, ALU.mult)
            dve.drain()
            parts = cst[:, 0:4 * KT].rearrange("p (k q) -> p k q", q=4)
            for k in range(2):
                x = small[:, 32 + 16 * k:48 + 16 * k]
                nc.vector.tensor_copy(parts[:, :, 2 * k], x)
                dve.drain()
                nc.vector.tensor_tensor(parts[:, :, 2 * k + 1], x, parts[:, :, 2 * k].bitcast(F32), ALU.subtract)
            dve.drain().then_inc(setup_dve, 1)
            dve.wait_ge(setup_in, 16 * N_SETUP)
            for k in range(2):
                nc.vector.tensor_tensor(lam4[:, 2 * k, :], lam4[:, 2 * k, :], lam4[:, 2 * k + 1, :], ALU.mult)
            dve.drain()
            nc.vector.tensor_reduce(small[:, 8:10], lam4[:, :, :].rearrange("p (a b) d -> p a b d", b=2)[:, :, 0, :],
                                    AX_X, ALU.add)
            dve.drain().then_inc(setup_dve, 1)
            dve.wait_ge(setup_act, 3)
            nc.vector.tensor_tensor(small[:, 12:13], small[:, 11:12], small[:, 10:11], ALU.subtract)
            dve.drain()
            nc.vector.tensor_scalar(small[:, 12:13], small[:, 12:13], -LAMBDA_INIT, None, ALU.add)
            nc.vector.tensor_scalar(gsub[:, :], gsub[:, :], 1.0 - LAMBDA_INIT, None, ALU.mult)
            for kt in range(AHEAD):
                split_lo(0, kt)
            split_chunk(0)
            ada_rows(0)
            with dve.Fori(1, 8) as i:
                split_chunk(i, lambda kt: ada_columns(i - 1, 0, i - 1) if kt == 2 else None)
                ada_rows(i)
            ada_columns(7, 0, 7)
            scale_columns(0)
            dve.wait_ge(sq_done, 5)
            row_norms(partial=False)
            for k in range(FEED):
                feed_step(0, k)
            split_chunk(C_L0, feed_beside(0))
            split_chunk(C_L0 + 1)
            first_norm = norm_head(dve, 0)
            split_chunk(C_L0 + 2, lambda kt: next(first_norm, None) if 4 <= kt < 9 else None)

            def pair0(i, pace, gate=False, order=None, tiles=(), last_head=False):
                split_chunk(i * 2 + C_L0I)
                ada_rows(i * 2 + C_L0I)
                steps = attention_dve(dve, L0, i, order, tiles, last_head)
                split_chunk(i * 2 + (C_L0I + 1), stepper(steps, pace, first=lambda: ada_columns(i + 8, 1, i)))
                finish(steps)
                if gate:
                    evacuate_gate(i * 2 + (C_L0I + 1), i + 3, i - 4)

            with dve.Fori(0, 4) as i:
                pair0(i, pace0)
            with dve.Fori(4, 7) as i:
                pair0(i, pace0s, True, ORDER0S, [i - 4])
            pair0(7, pace0t, True, ORDER0T, [3, 4], last_head=True)
            scale_columns(1)

            def multiply(c, t):
                dve.wait_ge(acc_ready, c * 5 + (t + 1 + ACC_CREDIT))
                nc.vector.tensor_tensor(stage[:, t, :], ps[:, t, :], gate_b[:, t // TS, :],
                                        ALU.mult).then_inc(acc_free, 1)

            def add_old(n, t):
                if t == 0:
                    dve.drain()
                    dve.wait_ge(xo_in, n * 32 + 32)
                nc.vector.tensor_tensor(stage[:, t, :], stage[:, t, :], x_old[:, t, :], ALU.add).then_inc(out_done, 1)
                if t == TT - 1:
                    dve.drain().then_inc(xo_free, 1)
                    dve.drain().then_inc(stage_full, 1)

            def output(first, F, n0, m0, last):
                last_norm = norm_out(dve) if F == 3 else iter(())
                split_chunk(first, lambda kt: next(last_norm, None))
                dve.wait_ge(S[F // 2].o_free, (8 if F == 1 else 16) + 1)
                ada_rows(first)
                ada_gate(m0, n0)
                for k in range(FEED):
                    feed_step(F, k)
                split_chunk(first + 1, feed_beside(F))
                dve.drain()
                for t in range(TT):
                    multiply(first + 1, t)

                def output_pair(j, last=False):
                    split_chunk(j * 2 + first)
                    ada_rows(j * 2 + first)

                    def beside(kt):
                        if kt == 0:
                            ada_gate(j + m0, j + n0)
                        elif kt < 6:
                            add_old(j + (n0 - 1), kt - 1)

                    split_chunk(j * 2 + (first + 1), beside, last)
                    dve.drain()
                    dve.wait_ge(stage_free, j + (11 if F == 1 else 31) + 1)
                    dve.wait_ge(sq_done, j * TT + (n0 * TT + TT))
                with dve.Fori(1, 3) as j:
                    output_pair(j)
                    for t in range(TT):
                        multiply(j * 2 + (first + 1), t)
                output_pair(3, last)
                dve.wait_ge(xo_in, (n0 + 3) * 32 + 32)
                for t in range(TT + 1):
                    if t < TT:
                        multiply(first + 7, t)
                    dve.drain()
                    if t > 0:
                        add_old(n0 + 3, t - 1)
                dve.wait_ge(sq_done, TT + (n0 + 4) * TT)
                row_norms(partial=True)

            output(C_O0, 1, 0, 16, False)
            for k in range(FEED):
                feed_step(2, k)
            split_chunk(C_L1, feed_beside(2))
            with dve.Fori(1, 3) as i:
                split_chunk(i + C_L1)
            nc.vector.memset(o_head[:, :, :], 0.0)
            with dve.Fori(0, 3) as g:
                steps = heads_dve(dve, g * 4, 4)
                for n in range(3):
                    split_chunk(g * 3 + (C_L1 + 3 + n), stepper(steps, pace1, n))
                finish(steps)
            with dve.Fori(0, 4) as j:
                steps = heads_dve(dve, j + 12, 1)
                split_chunk(j + (C_L1 + 12), stepper(steps, pace1g))
                finish(steps)
                evacuate_gate(j + (C_L1 + 12), j + 27, j + 4)
            output(C_O1, 3, 4, 20, True)
            dve.wait_ge(fg_in, 16)
            for j in range(4):
                if j < 3:
                    dve.wait_ge(fin_in[j], 16)
                for t in range(TT):
                    x = last_x[j][:, t, :]
                    last_op = nc.vector.scalar_tensor_tensor(x, x, rstd[:, t:t + 1], last_g[:, j * NC:(j + 1) * NC],
                                                             ALU.mult, ALU.mult)
                last_op.then_inc(fin_ready, 1)

        @block.gpsimd
        def _(pool):
            def wait(s, value):
                pool.wait_ge(s, value)
                pool.sem_inc(pool_passed, 1)

            def z_at(l, i):
                return z_d[l][i] if isinstance(i, int) else z_d[l][bass.ds(i, 1)].squeeze(0)

            def load_qk(L, h):
                s = S[L.n]
                z = z_d[L.n]
                if L.n == 0:
                    q = z_at(0, h // 4 + 1)[:, :, bass.ds((h % 4) * P, P)]
                    k = z[0, :, :, bass.ds(h // 4 * P, P)]
                    ck = a["cache_k0"][0].rearrange("t h d -> t (h d)")[:, bass.ds(h // 4 * P, P)]
                else:
                    q, k = (z_at(1, h // 4 * 3 + n)[:, :, bass.ds((h % 4) * P, P)] for n in range(2))
                    ck = a["cache_k1"][0].rearrange("t h m d -> t (h m d)")[:, bass.ds(h * P, P)]
                for dst, src in ((q_in[:, :, :], q), (k_in[:, :, :], k), (ck_in[:, :], ck)):
                    pool.dma_start(dst, src).then_inc(s.qk_in, 16)

            def load_v(L, h):
                s = S[L.n]
                if L.n == 0:
                    v = z_d[0][0, :, :, bass.ds(h // 4 * P + 256, P)]
                    cv = a["cache_v0"][0].rearrange("t h d -> t (h d)")[:, bass.ds(h // 4 * P, P)]
                else:
                    v = z_at(1, h // 4 * 3 + 2)[:, :, bass.ds((h % 4) * P, P)]
                    cv = a["cache_v1"][0].rearrange("t h d -> t (h d)")[:, bass.ds(h * P, P)]
                for dst, src in ((v_in[:, :, :], v), (cv_in[:, :], cv)):
                    pool.dma_start(dst, src).then_inc(s.v_in, 16)

            def rotate_head(L, h):
                s = S[L.n]
                if L.n == 0:
                    wait(s.normed, h + 1)
                else:
                    wait(s.qk_in, h * 48 + 48)
                half = L.dk // 4
                halves = "p (x s j) -> p x s j"
                for z in (q_in, k_in):
                    flat = z[:, 0:TS, :].rearrange("p t d -> p (t d)")
                    nc.gpsimd.tensor_tensor(rope_a[:, :], flat, rope_c[:, :], ALU.mult)
                    z4 = flat.rearrange(halves, s=2, j=half)
                    b4 = rope_b[:, :].rearrange(halves, s=2, j=half)
                    s4 = rope_s[:, :].rearrange(halves, s=2, j=half)
                    for k in range(2):
                        nc.gpsimd.tensor_tensor(b4[:, :, k, :], z4[:, :, 1 - k, :], s4[:, :, k, :], ALU.mult)
                    pool.drain()
                    nc.gpsimd.tensor_tensor(flat, rope_a[:, :], rope_b[:, :], ALU.add)
                    pool.drain()
                pool.drain().then_inc(s.roped, 1)
                if L.n == 0:
                    pool.dma_start(kn_d[h] if isinstance(h, int) else kn_d[bass.ds(h, 1)].squeeze(0),
                                   k_in[:, TS, :]).then_inc(kn_stored, 16)

            def next_qk(L, h):
                wait(S[L.n].t_ready, h * L.n_turn + (3 - L.n_turn))
                if L.n == 0:
                    wait(kn_stored, h * 16)
                load_qk(L, h)

            def next_v(L, h):
                wait(S[L.n].v_split, h)
                load_v(L, h)

            def store_head(L, h):
                wait(S[L.n].o_done, h + (1 if L.n == 0 else 2))
                at = h * P + (1024 if L.n == 0 else 0)
                pool.dma_start(o_d[L.n].rearrange("t p n -> p t n")[:, :, bass.ds(at, P)],
                               o_head[:, :, :]).then_inc(S[L.n].o_stored, 16)

            def free_head(L, h):
                wait(S[L.n].o_stored, h * 16 + 16)
                pool.sem_inc(S[L.n].o_free, 1)

            def store_stage(n, dst):
                wait(stage_full, n + 1)
                pool.dma_start(dst, stage[:, :, :]).then_inc(stage_stored, 16)

            def free_stage(n):
                wait(stage_stored, n * 16 + 16)
                pool.sem_inc(stage_free, 1)

            def load_spatial(t, buf, arrived):
                for n in range(4):
                    idx = (5, 6, 3, 4)[n]
                    if n % 2 == 0:
                        z = z_d[0].rearrange("i p t n -> t p i n")
                        z = z[t] if isinstance(t, int) else z[bass.ds(t, 1)].squeeze(0)
                        pool.dma_start(buf[:, n * NC:(n + 2) * NC].rearrange("p (i n) -> p i n", i=2),
                                       z[:, idx:idx + 2, :]).then_inc(arrived, 16)

            def store_spatial(t, buf):
                wait(sp_free, t * 2 + 2)
                o = o_d[0][t] if isinstance(t, int) else o_d[0][bass.ds(t, 1)].squeeze(0)
                pool.dma_start(o[:, 0:1024], buf[:, 1024:2048]).then_inc(sp_stored, 16)

            pool.sem_inc(stage_free, 1)
            for s in S:
                pool.sem_inc(s.o_free, 1)
            xs = a["x_sample"][0].rearrange("(t p) d -> t p d", p=P)
            pool.dma_start(area[:, 2, :], xs[0]).then_inc(xt_in, 16)
            for t in range(1, TT):
                wait(sq_done, t)
                pool.dma_start(area[:, 2, :], xs[t] if t < TS else a["x_prompt"][0]).then_inc(xt_in, 16)
            wait(sq_done, 5)

            def load_x(F, b, sample, prompt):
                cols = slice(b * NC, (b + 1) * NC)
                pool.dma_start(slot(F, b)[:, 0:TS, :], sample[:, :, cols]).then_inc(x_in[b % 2], 16)
                pool.dma_start(slot(F, b)[:, TS, :], prompt[:, cols]).then_inc(x_in[b % 2], 16)

            def feed_x(F, sample, prompt):
                for b in range(4):
                    if b >= 2:
                        wait(turn_ready, 16 * F + 4 * (b - 1))
                    load_x(F, b, sample, prompt)

            x0 = (xs.rearrange("t p d -> p t d"), a["x_prompt"][0])
            feed_x(0, *x0)
            store_stage(0, z_at(0, 0))
            free_stage(0)
            store_stage(1, z_at(0, 1))
            free_stage(1)
            load_qk(L0, 0)
            load_v(L0, 0)
            rotate_head(L0, 0)
            store_stage(2, z_at(0, 2))
            free_stage(2)

            def pair0(i, tiles=(), hold=False):
                if tiles:
                    load_spatial(tiles[0], sp_bufs[0], sp_in)
                next_qk(L0, i + 1)
                next_v(L0, i + 1)
                if tiles:
                    store_spatial(tiles[0], sp_bufs[0])
                    wait(sp_stored, tiles[0] * 16 + 16)
                    pool.sem_inc(stage_free, 1)
                rotate_head(L0, i + 1)
                store_head(L0, i)
                free_head(L0, i)
                store_stage(i + 3, z_at(0, i + 3))
                if hold:
                    wait(stage_stored, (i + 3) * 16 + 16)
                else:
                    free_stage(i + 3)

            with pool.Fori(0, 3) as i:
                pair0(i)
            pair0(3, hold=True)
            with pool.Fori(4, 7) as i:
                pair0(i, [i - 4], hold=True)

            def load_bias(l, j):
                pool.dma_start(gate_bias, a[f"b_ada{l}"][bass.ds(j * NC + 2 * D, NC)].unsqueeze(0)
                               .to_broadcast([P, NC])).then_inc(gb_in, 16)

            def load_y(l, b):
                pool.dma_start(blk[b % 2], o_d[l].rearrange("t p n -> p t n")[:, :, b * NC:(b + 1) * NC]).then_inc(
                    o_in[b % 2], 16)

            def load_g(l, b):
                pool.dma_start(stage[:, :, :] if b > 0 else blk[1],
                               z_d[l][b + (7 if l == 0 else 12)]).then_inc(g_in, 16)

            def load_old(src, j):
                col = bass.ds(j * NC, NC)
                pool.dma_start(x_old[:, 0:TS, :], src[0][:, :, col]).then_inc(xo_in, 16)
                pool.dma_start(x_old[:, TS, :], src[1][:, col]).then_inc(xo_in, 16)

            load_spatial(3, sp_bufs[0], sp_in)
            load_bias(0, 0)
            wait(S[0].v_split, 8)
            load_spatial(4, sp_bufs[1], sp_last_in)
            store_spatial(3, sp_bufs[0])
            wait(sp_stored, 64)
            pool.sem_inc(stage_free, 1)
            store_spatial(4, sp_bufs[1])
            wait(sp_stored, 80)
            load_y(0, 0)
            wait(S[0].t_ready, 80)
            load_g(0, 0)
            store_head(L0, 7)
            free_head(L0, 7)
            store_stage(10, z_at(0, 10))
            free_stage(10)

            def feed_y(l, F):
                for b in range(1, 4):
                    wait(src_ready, 4 * F + b)
                    if b >= 2:
                        wait(turn_ready, 16 * F + 4 * (b - 1))
                    load_y(l, b)
                    load_g(l, b)
                wait(turn_ready, 16 * F + 12)

            wait(kn_stored, 16 * 8)
            for t, n in ((rope_c, 0), (rope_s, 1)):
                pool.dma_start(t[:, :], a["rope"][1, n]).then_inc(copied, 16)
            for g in range(2):
                pool.dma_start(new_k0[0][:, g, :], kn_d[4 * g]).then_inc(copied, 16)
            pool.dma_start(new_v0[0].rearrange("t h d -> t (h d)"), z_d[0][0, :, TS, 256:512]).then_inc(copied, 16)

            def output(l, F, n0, s0, src, dst):
                feed_y(l, F)
                load_old(src, 0)
                wait(gb_free, n0 + 1)
                load_bias(l, 1)
                dst = dst.rearrange("t p d -> p t d")

                def output_chunk(j, bias):
                    wait(xo_free, j + (n0 + 1))
                    load_old(src, j + 1)
                    store_stage(j + s0, dst[:, :, bass.ds(j * NC, NC)])
                    if bias:
                        wait(gb_free, j + (n0 + 2))
                        load_bias(l, j + 2)
                    free_stage(j + s0)

                with pool.Fori(0, 2) as j:
                    output_chunk(j, True)
                output_chunk(2, False)
                if l == 0:
                    load_x(2, 0, *x1)
                else:
                    pool.dma_start(last_x[2], x2_d.rearrange("t p d -> p t d")[:, :, 2 * NC:3 * NC]).then_inc(
                        fin_in[2], 16)
                    wait(w_lo_ready, C_END * KT - KT + 2 * 2)
                    pool.dma_start(last_g, a["final_g"].unsqueeze(0).to_broadcast([P, D])).then_inc(fg_in, 16)
                    for k, used in enumerate((5, 8)):
                        wait(w_lo_ready, C_END * KT - KT + 2 * used)
                        pool.dma_start(last_x[k], x2_d.rearrange("t p d -> p t d")[:, :, k * NC:(k + 1) * NC]).then_inc(
                            fin_in[k], 16)
                    return
                wait(xo_free, n0 + 4)
                store_stage(s0 + 3, dst[:, :, 3 * NC:4 * NC])

            x1 = (x_d.rearrange("t p d -> p t d")[:, 0:TS, :], x_d[TS])
            output(0, 1, 0, 11, x0, x_d)
            load_x(2, 1, *x1)
            free_stage(14)
            for b in (2, 3):
                wait(turn_ready, 32 + 4 * (b - 1))
                load_x(2, b, *x1)
            wait(copied, 16 * 5)
            for n in range(2):
                store_stage(15 + n, z_at(1, n))
                free_stage(15 + n)
            load_qk(L1, 0)
            rotate_head(L1, 0)
            store_stage(17, z_at(1, 2))
            free_stage(17)
            load_v(L1, 0)

            def head1(h, first=False, v=True):
                next_qk(L1, h + 1)
                rotate_head(L1, h + 1)
                if v:
                    next_v(L1, h + 1)
                if not first:
                    store_head(L1, h - 1)
                    free_head(L1, h - 1)

            def group1(g, first=False):
                for x in range(4):
                    head1(g * 4 + x, first and x == 0, x < 3)
                    if x > 0:
                        store_stage(g * 3 + (17 + x), z_at(1, g * 3 + (2 + x)))
                        free_stage(g * 3 + (17 + x))
                next_v(L1, g * 4 + 4)

            group1(0, first=True)
            with pool.Fori(1, 3) as g:
                group1(g)
            with pool.Fori(0, 3) as j:
                head1(j + 12)
                store_stage(j + 27, z_at(1, j + 12))
                free_stage(j + 27)
            wait(gb_free, 4)
            load_bias(1, 0)
            wait(S[1].v_split, 16)
            load_y(1, 0)
            store_head(L1, 14)
            free_head(L1, 14)
            wait(S[1].t_ready, 160)
            load_g(1, 0)
            store_stage(30, z_at(1, 15))
            store_head(L1, 15)
            free_head(L1, 15)
            free_stage(30)
            for g in range(4):
                heads = slice(4 * g, 4 * g + 4)
                pool.dma_start(new_k1[0][:, heads].rearrange("t h m d -> t (h m d)"),
                               z_d[1][3 * g + 1, :, TS, :]).then_inc(copied, 16)
                pool.dma_start(new_v1[0][:, heads].rearrange("t h d -> t (h d)"),
                               z_d[1][3 * g + 2, :, TS, :]).then_inc(copied, 16)
            output(1, 3, 4, 31, x1, x2_d)
            for j in range(4):
                wait(fin_ready, j + 1)
                cols = slice(j * NC, (j + 1) * NC)
                pool.dma_start(y_sample[0].rearrange("(t p) d -> p t d", p=P)[:, :, cols],
                               last_x[j][:, 0:TS, :]).then_inc(fin_stored, 16)
                pool.dma_start(y_prompt[0][:, cols], last_x[j][:, TS, :]).then_inc(fin_stored, 16)
            wait(fin_stored, 128)
            wait(copied, 16 * 13)


def shape_constants():
    import numpy as np
    layout = np.zeros((P, 386), np.float32)
    layout[:, 0:128] = np.eye(P, dtype=np.float32)
    layout[0:2, 128:256] = 1.0
    layout[2:4, 256:384] = 1.0
    layout[0:2, 384] = 1.0
    layout[2:4, 385] = 1.0
    rope = np.zeros((2, 2, P, TS * P), np.float32)
    tok = np.arange(TS * P)
    pos = [(tok // 64).astype(np.float32), (tok % 64).astype(np.float32)]
    for l, dk in enumerate((128, 64)):
        half = dk // 4
        freqs = np.float32(10000.0) ** (-np.arange(half, dtype=np.float32) / np.float32(half))
        cols = []
        for axis in range(2):
            ang = pos[axis][:, None] * freqs[None, :]
            cols.append((np.cos(ang), np.sin(ang)))
        c = np.concatenate([np.concatenate([x, x], 1) for x, _ in cols], 1)
        s = np.concatenate([np.concatenate([-x, x], 1) for _, x in cols], 1)
        for n, tab in enumerate((c, s)):
            tab = np.tile(tab, (1, P // dk)).astype(np.float32)
            rope[l, n] = tab.reshape(TS, P, P).transpose(1, 0, 2).reshape(P, TS * P)
    return {"layout": layout, "rope": rope}


_INS = ["x_prompt", "x_sample", "cache_k0", "cache_v0", "cache_k1", "cache_v1", "c", "c_ctx",
        "w_ada0", "b_ada0", "norm_g0", "w_in0", "w_s0", "b_s0", "q_norm_g0", "k_norm_g0", "w_out0",
        "w_ada1", "b_ada1", "norm_g1", "w_in1", "lambda_q1", "lambda_k1", "lambda_q2", "lambda_k2",
        "subln_g1", "w_out1", "final_g"]
_OUTS = [(1, 128, 2048), (1, 512, 2048), (1, 128, 2, 128), (1, 128, 2, 128), (1, 128, 16, 2, 64), (1, 128, 16, 128)]


def kernel(**inputs):
    import numpy as _np
    import concourse.bacc as _bacc
    from concourse import mybir as _mybir
    from concourse.bass_utils import run_bass_kernel_spmd as _run

    nc = _bacc.Bacc("TRN2", target_bir_lowering=False, num_devices=1)
    arrays, a = {}, {}
    given = {name: _np.ascontiguousarray(inputs[name]) for name in _INS}
    for name, x in {**given, **shape_constants()}.items():
        arrays[f"in_{name}_dram"] = x
        a[name] = nc.dram_tensor(f"in_{name}_dram", x.shape, _mybir.dt.from_np(x.dtype), kind="ExternalInput").ap()
    outs = [nc.dram_tensor(f"out_{i}_dram", shape, _mybir.dt.float32, kind="ExternalOutput").ap()
            for i, shape in enumerate(_OUTS)]
    kernel_program(nc, a, outs)
    r = _run(nc, [arrays], core_ids=[0])
    return tuple(r.results[0][f"out_{i}_dram"] for i in range(len(_OUTS)))
```
